# Optimizing a Trainium2 kernel written in Bass

```python
import jax, jax.numpy as jnp
from jax import lax
import numpy as np
import math

D_MODEL = 1024
BATCH = 1
SEQ = 512
DEPTH = 1

ATTN_HEADS = 8
HEAD_DIM = 64
ATTN_WIDTH = ATTN_HEADS * HEAD_DIM
CONV_WIDTH = D_MODEL - ATTN_WIDTH
CONV_KERNEL = 31
D_FF = 2816
FFN_KERNEL = 3
BLOCK_Q = 128
IN_WIDTH = 3 * ATTN_WIDTH + 2 * CONV_WIDTH
EPS = 1e-6


def rms_norm(x, g):
    xf = x.astype(jnp.float32)
    y = xf * lax.rsqrt(jnp.mean(xf * xf, axis=-1, keepdims=True) + EPS)
    return (y * g.astype(jnp.float32)).astype(x.dtype)

def layer_norm(x, g, b):
    xf = x.astype(jnp.float32)
    mu = jnp.mean(xf, axis=-1, keepdims=True)
    xc = xf - mu
    var = jnp.mean(xc * xc, axis=-1, keepdims=True)
    y = xc * lax.rsqrt(var + EPS) * g.astype(jnp.float32) + b.astype(jnp.float32)
    return y.astype(x.dtype)

def causal_depthwise_conv(x, w, b):
    k_width, channels = w.shape
    y = lax.conv_general_dilated(
        x, w[:, None, :].astype(x.dtype),
        window_strides=(1,), padding=[(k_width - 1, 0)],
        dimension_numbers=("NWC", "WIO", "NWC"),
        feature_group_count=channels)
    return y + b.astype(x.dtype)

def stick_breaking_attention(q, k, v):
    seq = q.shape[1]
    scale = q.shape[-1] ** -0.5
    outs = []
    for start in range(0, seq, BLOCK_Q):
        end = min(start + BLOCK_Q, seq)
        qb = q[:, start:end].astype(jnp.float32)
        kb = k[:, :end].astype(jnp.float32)
        vb = v[:, :end].astype(jnp.float32)
        z = jnp.einsum("bqhd,bkhd->bhqk", qb, kb) * scale
        t_idx = start + jnp.arange(end - start)[:, None]
        s_idx = jnp.arange(end)[None, :]
        mask = s_idx < t_idx
        log_beta = jax.nn.log_sigmoid(z)
        log_one_minus = jnp.where(mask, jax.nn.log_sigmoid(-z), 0.0)
        tail = lax.cumsum(log_one_minus, axis=3, reverse=True) - log_one_minus
        weights = jnp.where(mask, jnp.exp(log_beta + tail), 0.0)
        outs.append(jnp.einsum("bhqk,bkhd->bqhd", weights, vb))
    return jnp.concatenate(outs, axis=1).astype(v.dtype)

def first_inputs(seed: int = 0) -> dict:
    key = jax.random.key(seed)
    ks = jax.random.split(key, 16)
    f32 = jnp.float32
    out_scale = (2.0 * DEPTH) ** -0.5

    def nrm(k, shape, s):
        return jax.random.normal(k, shape, f32) * s

    return {
        "x": jax.random.normal(ks[0], (BATCH, SEQ, D_MODEL), f32),
        "norm1_g": 1.0 + nrm(ks[1], (DEPTH, D_MODEL), 0.02),
        "w_in": nrm(ks[2], (DEPTH, D_MODEL, IN_WIDTH), D_MODEL ** -0.5),
        "q_norm_g": 1.0 + nrm(ks[3], (DEPTH, HEAD_DIM), 0.02),
        "k_norm_g": 1.0 + nrm(ks[4], (DEPTH, HEAD_DIM), 0.02),
        "conv_dw_w": nrm(ks[5], (DEPTH, CONV_KERNEL, CONV_WIDTH), CONV_KERNEL ** -0.5),
        "conv_dw_b": nrm(ks[6], (DEPTH, CONV_WIDTH), 0.01),
        "conv_ln_g": 1.0 + nrm(ks[7], (DEPTH, CONV_WIDTH), 0.02),
        "conv_ln_b": nrm(ks[8], (DEPTH, CONV_WIDTH), 0.01),
        "w_out": nrm(ks[9], (DEPTH, D_MODEL, D_MODEL), D_MODEL ** -0.5 * out_scale),
        "norm2_g": 1.0 + nrm(ks[10], (DEPTH, D_MODEL), 0.02),
        "w_up": nrm(ks[11], (DEPTH, D_MODEL, 2 * D_FF), D_MODEL ** -0.5),
        "ffn_dw_w": nrm(ks[12], (DEPTH, FFN_KERNEL, D_FF), FFN_KERNEL ** -0.5),
        "ffn_dw_b": nrm(ks[13], (DEPTH, D_FF), 0.01),
        "w_down": nrm(ks[14], (DEPTH, D_FF, D_MODEL), D_FF ** -0.5 * out_scale),
    }

def first_block(x, norm1_g, w_in, q_norm_g, k_norm_g, conv_dw_w, conv_dw_b,
              conv_ln_g, conv_ln_b, w_out, norm2_g, w_up, ffn_dw_w, ffn_dw_b,
              w_down):
    bsz, seq, _ = x.shape
    splits = [ATTN_WIDTH, 2 * ATTN_WIDTH, 3 * ATTN_WIDTH, 3 * ATTN_WIDTH + CONV_WIDTH]
    for layer in range(DEPTH):
        h = rms_norm(x, norm1_g[layer])
        proj = h @ w_in[layer]
        q, k, v, glu_a, glu_b = jnp.split(proj, splits, axis=-1)
        q = rms_norm(q.reshape(bsz, seq, ATTN_HEADS, HEAD_DIM), q_norm_g[layer])
        k = rms_norm(k.reshape(bsz, seq, ATTN_HEADS, HEAD_DIM), k_norm_g[layer])
        v = v.reshape(bsz, seq, ATTN_HEADS, HEAD_DIM)
        attn = stick_breaking_attention(q, k, v).reshape(bsz, seq, ATTN_WIDTH)

        c = glu_a * jax.nn.sigmoid(glu_b)
        c = causal_depthwise_conv(c, conv_dw_w[layer], conv_dw_b[layer])
        c = jax.nn.silu(layer_norm(c, conv_ln_g[layer], conv_ln_b[layer]))

        mixed = jnp.concatenate([attn, c], axis=-1) @ w_out[layer]
        x = x + mixed

        h = rms_norm(x, norm2_g[layer])
        gate, val = jnp.split(h @ w_up[layer], 2, axis=-1)
        gate = jax.nn.silu(causal_depthwise_conv(gate, ffn_dw_w[layer], ffn_dw_b[layer]))
        x = x + (gate * val) @ w_down[layer]
    return x


MIX_WIDTH = D_MODEL
HG_HEADS = 4
HG_DK = 128
HG_DV = 128
HG_KEY_WIDTH = HG_HEADS * HG_DK
HG_VAL_WIDTH = HG_HEADS * HG_DV
HG_CHUNK = 64
ATT_HEADS = 8
ATT_KV_HEADS = 2
ATT_GROUP = ATT_HEADS // ATT_KV_HEADS
ATT_HD = 64
ATT_Q_WIDTH = ATT_HEADS * ATT_HD
ATT_KV_WIDTH = ATT_KV_HEADS * ATT_HD
WINDOW = 128
ATT_BLOCK = 128
HG_COLS = 2 * HG_KEY_WIDTH + 2 * HG_VAL_WIDTH
ATT_COLS = ATT_Q_WIDTH + 2 * ATT_KV_WIDTH
IN_COLS = HG_COLS + ATT_COLS
CONV_W = 3


def rmsnorm(x, w, eps=EPS):
    xf = x.astype(jnp.float32)
    inv = lax.rsqrt(jnp.mean(xf * xf, axis=-1, keepdims=True) + eps)
    return (xf * inv * w.astype(jnp.float32)).astype(x.dtype)

def hgrn2_chunkwise(q, k, v, log_f):
    B, S, H, DK = q.shape
    DV = v.shape[-1]
    n = S // HG_CHUNK

    def to_chunks(a):
        return a.astype(jnp.float32).reshape(B, n, HG_CHUNK, H, a.shape[-1]).transpose(1, 0, 3, 2, 4)

    qc, kc, vc, gc = to_chunks(q), to_chunks(k), to_chunks(v), to_chunks(log_f)
    causal = jnp.tril(jnp.ones((HG_CHUNK, HG_CHUNK), dtype=bool))[:, :, None]

    def step(state, inp):
        qi, ki, vi, gi = inp
        b = jnp.cumsum(gi, axis=2)
        rel = b[:, :, :, None, :] - b[:, :, None, :, :]
        decay = jnp.exp(jnp.where(causal, rel, -jnp.inf))
        scores = jnp.einsum('bhtk,bhsk,bhtsk->bhts', qi, ki, decay)
        intra = jnp.einsum('bhts,bhsv->bhtv', scores, vi)
        inter = jnp.einsum('bhtk,bhkv->bhtv', qi * jnp.exp(b), state)
        b_last = b[:, :, -1:, :]
        new_state = state * jnp.exp(b_last)[:, :, 0, :, None] + jnp.einsum(
            'bhsk,bhsv->bhkv', ki * jnp.exp(b_last - b), vi)
        return new_state, intra + inter

    state0 = jnp.zeros((B, H, DK, DV), jnp.float32)
    _, out = lax.scan(step, state0, (qc, kc, vc, gc))
    return out.transpose(1, 0, 3, 2, 4).reshape(B, S, H, DV)

def sliding_window_attention_with_sinks(q, k, v, sinks):
    B, S = q.shape[0], q.shape[1]
    nb = S // ATT_BLOCK
    scale = 1.0 / math.sqrt(ATT_HD)
    qb = q.astype(jnp.float32).reshape(B, nb, ATT_BLOCK, ATT_KV_HEADS, ATT_GROUP, ATT_HD)

    def band_keys(a):
        ap = jnp.pad(a.astype(jnp.float32), ((0, 0), (ATT_BLOCK, 0), (0, 0), (0, 0)))
        ap = ap.reshape(B, nb + 1, ATT_BLOCK, ATT_KV_HEADS, ATT_HD)
        return jnp.concatenate([ap[:, :-1], ap[:, 1:]], axis=2)

    kb, vb = band_keys(k), band_keys(v)
    scores = jnp.einsum('bnqhgd,bnkhd->bnhgqk', qb, kb) * scale
    qi = jnp.arange(ATT_BLOCK)[:, None]
    kj = jnp.arange(2 * ATT_BLOCK)[None, :]
    dist = qi + ATT_BLOCK - kj
    band = (dist >= 0) & (dist < WINDOW)
    key_pos = jnp.arange(nb)[:, None] * ATT_BLOCK + jnp.arange(2 * ATT_BLOCK)[None, :] - ATT_BLOCK
    mask = band[None] & (key_pos >= 0)[:, None, :]
    scores = jnp.where(mask[None, :, None, None], scores, -jnp.inf)
    sink = sinks.astype(jnp.float32).reshape(ATT_KV_HEADS, ATT_GROUP)[None, None, :, :, None, None]
    m = jnp.maximum(jnp.max(scores, axis=-1, keepdims=True), sink)
    p = jnp.exp(scores - m)
    denom = jnp.sum(p, axis=-1, keepdims=True) + jnp.exp(sink - m)
    out = jnp.einsum('bnhgqk,bnkhd->bnqhgd', p / denom, vb)
    return out.reshape(B, S, ATT_HEADS * ATT_HD)

def causal_depthwise_conv_2(a, w, b):
    C = a.shape[-1]
    y = lax.conv_general_dilated(
        a, w[:, None, :].astype(a.dtype), window_strides=(1,), padding=[(CONV_W - 1, 0)],
        dimension_numbers=('NWC', 'WIO', 'NWC'), feature_group_count=C)
    return y + b.astype(a.dtype)

def second_inputs(seed: int = 0) -> dict:
    key = jax.random.key(seed)
    ks = jax.random.split(key, 16)
    f32 = jnp.float32
    nrm = lambda k, shape, s: jax.random.normal(k, shape, f32) * s
    return {
        "x": jax.random.normal(ks[0], (BATCH, SEQ, D_MODEL), f32),
        "norm_mix_w": 1.0 + nrm(ks[1], (DEPTH, D_MODEL), 0.02),
        "w_in": nrm(ks[2], (DEPTH, D_MODEL, IN_COLS), D_MODEL ** -0.5),
        "b_attn": nrm(ks[3], (DEPTH, ATT_COLS), 0.02),
        "lb_logits": nrm(ks[4], (DEPTH + 1, HG_KEY_WIDTH), 0.1),
        "hg_norm_w": 1.0 + nrm(ks[5], (DEPTH, HG_DV), 0.02),
        "sinks": nrm(ks[6], (DEPTH, ATT_HEADS), 0.5),
        "w_out": nrm(ks[7], (DEPTH, MIX_WIDTH, D_MODEL), MIX_WIDTH ** -0.5),
        "norm_ffn_w": 1.0 + nrm(ks[8], (DEPTH, D_MODEL), 0.02),
        "w_gate": nrm(ks[9], (DEPTH, D_MODEL, D_FF), D_MODEL ** -0.5),
        "w_up": nrm(ks[10], (DEPTH, D_MODEL, D_FF), D_MODEL ** -0.5),
        "conv_w": nrm(ks[11], (DEPTH, CONV_W, D_FF), CONV_W ** -0.5),
        "conv_b": nrm(ks[12], (DEPTH, D_FF), 0.02),
        "w_down": nrm(ks[13], (DEPTH, D_FF, D_MODEL), D_FF ** -0.5),
        "final_norm_w": 1.0 + nrm(ks[14], (D_MODEL,), 0.02),
    }

def second_block(x, norm_mix_w, w_in, b_attn, lb_logits, hg_norm_w, sinks, w_out,
              norm_ffn_w, w_gate, w_up, conv_w, conv_b, w_down, final_norm_w):
    B, S, _ = x.shape
    lb_all = jnp.cumsum(jax.nn.softmax(lb_logits.astype(jnp.float32), axis=0), axis=0)[:DEPTH]
    h = x
    for l in range(DEPTH):
        u = rmsnorm(h, norm_mix_w[l])
        proj = u @ w_in[l]
        hq, hf, hi, hg, att = jnp.split(
            proj, [HG_KEY_WIDTH, 2 * HG_KEY_WIDTH, 2 * HG_KEY_WIDTH + HG_VAL_WIDTH, HG_COLS], axis=-1)
        lb = lb_all[l]
        f = lb + (1.0 - lb) * jax.nn.sigmoid(hf.astype(jnp.float32))
        log_f = jnp.log(f).reshape(B, S, HG_HEADS, HG_DK)
        k_hg = (1.0 - f).reshape(B, S, HG_HEADS, HG_DK)
        q_hg = hq.astype(jnp.float32).reshape(B, S, HG_HEADS, HG_DK) * (HG_DK ** -0.5)
        v_hg = hi.reshape(B, S, HG_HEADS, HG_DV)
        o_hg = hgrn2_chunkwise(q_hg, k_hg, v_hg, log_f)
        o_hg = rmsnorm(o_hg, hg_norm_w[l]).reshape(B, S, HG_VAL_WIDTH)
        o_hg = (o_hg * jax.nn.silu(hg.astype(jnp.float32))).astype(h.dtype)
        att = att + b_attn[l]
        aq, ak, av = jnp.split(att, [ATT_Q_WIDTH, ATT_Q_WIDTH + ATT_KV_WIDTH], axis=-1)
        o_att = sliding_window_attention_with_sinks(
            aq.reshape(B, S, ATT_HEADS, ATT_HD),
            ak.reshape(B, S, ATT_KV_HEADS, ATT_HD),
            av.reshape(B, S, ATT_KV_HEADS, ATT_HD),
            sinks[l]).astype(h.dtype)
        mix = jnp.concatenate([o_hg, o_att], axis=-1)
        h = h + mix @ w_out[l]
        v = rmsnorm(h, norm_ffn_w[l])
        gate = causal_depthwise_conv_2(v @ w_gate[l], conv_w[l], conv_b[l])
        h = h + (jax.nn.silu(gate) * (v @ w_up[l])) @ w_down[l]
    return rmsnorm(h, final_norm_w)


def setup_inputs(seed=0):
    out = dict(first_inputs(seed))
    for name, value in second_inputs(seed + 1).items():
        if name != "x":
            out[name + "_2"] = value
    return out


def reference(
    x, norm1_g, w_in, q_norm_g, k_norm_g, conv_dw_w, conv_dw_b, conv_ln_g, conv_ln_b, w_out,
    norm2_g, w_up, ffn_dw_w, ffn_dw_b, w_down, norm_mix_w_2, w_in_2, b_attn_2, lb_logits_2,
    hg_norm_w_2, sinks_2, w_out_2, norm_ffn_w_2, w_gate_2, w_up_2, conv_w_2, conv_b_2, w_down_2,
    final_norm_w_2,
):
    x = first_block(
        x, norm1_g, w_in, q_norm_g, k_norm_g, conv_dw_w, conv_dw_b, conv_ln_g, conv_ln_b, w_out,
        norm2_g, w_up, ffn_dw_w, ffn_dw_b, w_down,
    )
    return second_block(
        x, norm_mix_w_2, w_in_2, b_attn_2, lb_logits_2, hg_norm_w_2, sinks_2, w_out_2,
        norm_ffn_w_2, w_gate_2, w_up_2, conv_w_2, conv_b_2, w_down_2, final_norm_w_2,
    )


_drawn_inputs = setup_inputs


def setup_inputs(seed=0):
    import zlib

    import numpy as np

    out = dict(_drawn_inputs(seed))
    spreads = {}
    factors = {'norm1_g': 3.983,
     'q_norm_g': 8.0,
     'k_norm_g': 8.0,
     'conv_dw_b': 4.268,
     'conv_ln_g': 5.813,
     'conv_ln_b': 8.0,
     'norm2_g': 4.181,
     'ffn_dw_b': 8.0,
     'norm_mix_w_2': 3.323,
     'b_attn_2': 47.008,
     'hg_norm_w_2': 18.988,
     'sinks_2': 64.0,
     'norm_ffn_w_2': 12.406,
     'conv_b_2': 17.893,
     'final_norm_w_2': 22.957}
    for name, (base, spread) in spreads.items():
        noise = np.random.default_rng([zlib.crc32(name.encode()), seed]).standard_normal(out[name].shape)
        drawn = base * np.exp(spread * noise) if base else spread * noise
        out[name] = __import__('jax').numpy.asarray(drawn.astype(out[name].dtype))
    for name, factor in factors.items():
        out[name] = (out[name] * factor).astype(out[name].dtype)
    return out
```

```python
from contextlib import ExitStack

import concourse.bass as bass
from concourse import mybir

ALU = mybir.AluOpType
ACT = mybir.ActivationFunctionType
F32 = mybir.dt.float32
F32R = mybir.dt.float32r
I32 = mybir.dt.int32
AX = mybir.AxisListType

P = 128
SEQ = 512
TT = SEQ // P
DM = 1024
KD = DM // P
DFF = 2816
KF = DFF // P
NUP = KF // 2
EPS = 1e-6
CK = 31
CT = 4
PAD = CK - 1
NEG = -1e30

U_IN, U_OUT, U_UP, U_DOWN = 0, 20, 28, 72
U_IN2, U_OUT2, U_UP2, U_DOWN2, U_END = 94, 116, 124, 168, 190

C_N1, C_N2, C_NM, C_NF = 0, 8, 16, 24
C_CB, C_LG, C_LB, C_LL, C_HG = 32, 36, 40, 44, 52
C_FB, C_FB2, C_QG, C_KG, C_BA, C_FN = 53, 75, 97, 98, 99, 105
PROWS = (113, 66, 66, 124)
NPROW = 20

AH = 8
GC = 27
FILL = (1, 3, 5, 7, 15, 19, 23, 27)
STATS = (0, 4, 12, 24, 32)

OUT_ORDER = (0, 1, 2, 3, 5, 6, 7, 4)

ZOFF = (0, 640, 1024, 512)
ZLEN = (512, 384, 256, 128)
ZW = 1280


def hybrid_blocks_kernel(
    nc, x, norm1_g, w_in, q_norm_g, k_norm_g, conv_dw_w, conv_dw_b, conv_ln_g, conv_ln_b, w_out,
    norm2_g, w_up, ffn_dw_w, ffn_dw_b, w_down, norm_mix_w_2, w_in_2, b_attn_2, lb_logits_2,
    hg_norm_w_2, sinks_2, w_out_2, norm_ffn_w_2, w_gate_2, w_up_2, conv_w_2, conv_b_2, w_down_2,
    final_norm_w_2, out,
):
    with ExitStack() as ctx:
        def sb(name, shape, dt=F32, stack=ctx):
            return stack.enter_context(nc.sbuf_tensor(name, shape, dt))

        def sem(name):
            return ctx.enter_context(nc.semaphore(name))

        xT = sb("xT", [P, KD, SEQ])
        h_hi = sb("h_hi", [P, KD, SEQ], F32R)
        h_lo = sb("h_lo", [P, KD, SEQ], F32R)
        w_raw = sb("w_raw", [P, 2, 2 * DM])
        w_hi = sb("w_hi", [P, 4, DM], F32R)
        w_lo = sb("w_lo", [P, 4, DM], F32R)
        ident = sb("ident", [P, P])
        ones = sb("ones", [P, P])
        par = sb("par", [P, 4, P])
        stat = sb("stat", [P, 4])
        rstd = sb("rstd", [P, 4])
        ss0 = sb("ss0", [P, 4])
        sinkb = sb("sinkb", [P, 8])
        mhalf = sb("mhalf", [P, 4])
        sq = sb("sq", [P, 2, SEQ])
        diag = sb("diag", [P, TT, P])
        htmp = sb("htmp", [P, 2, SEQ])

        with ExitStack() as early:
            glu = sb("glu", [P, CT, PAD + SEQ + 2], stack=early)
            cy = sb("cy", [P, CT, SEQ], stack=early)
            qk = sb("qk", [P, 8, SEQ], stack=early)
            vtok = sb("vtok", [P, TT, SEQ], stack=early)
            sel = sb("sel", [P, 8, 16], stack=early)
            selT = sb("selT", [16, 8, P], stack=early)
            nvar = sb("nvar", [16, 3, SEQ], stack=early)
            gq8 = sb("gq8", [P, 1], stack=early)
            lnone = sb("lnone", [P, P], stack=early)
            smask = sb("smask", [P, P], stack=early)
            nmask = sb("nmask", [P, P], stack=early)
            ntri_f = sb("ntri_f", [P, P], stack=early)
            ntri = sb("ntri", [P, P], F32R, stack=early)
            nones = sb("nones", [P, P], F32R, stack=early)
            with ExitStack() as start:
                xtok = sb("xtok", [P, TT, DM], stack=start)
                xjunk = sb("xjunk", [P, DM], stack=start)
                prow = sb("prow", [P, 4, P], stack=start)
            with ExitStack() as projecting:
                sqk = sb("sqk", [P, 8, SEQ], stack=projecting)
            zl = sb("zl", [P, 3, ZW], stack=early)
            sp_hi = sb("sp_hi", [P, 2, ZW], F32R, stack=early)
            sp_lo = sb("sp_lo", [P, 2, ZW], F32R, stack=early)
        with ExitStack() as mid:
            m_hi = sb("m_hi", [P, 4, SEQ], F32R, stack=mid)
            m_lo = sb("m_lo", [P, 4, SEQ], F32R, stack=mid)
            kT = sb("kT", [P, 2, SEQ], stack=mid)
            vT = sb("vT", [P, SEQ], stack=mid)
            vt2 = sb("vt2", [P, TT, P], stack=mid)
            aq = sb("aq", [P, 4, SEQ], stack=mid)
            kk = sb("kk", [P, 4, SEQ], stack=mid)
            qq = sb("qq", [P, 4, SEQ], stack=mid)
            bb = sb("bb", [P, 4, SEQ], stack=mid)
            vh = sb("vh", [P, TT, SEQ], stack=mid)
            lmask = sb("lmask", [P, 7, P], I32, stack=mid)
            cmask = sb("cmask", [P, SEQ], stack=mid)
            band = sb("band", [P, 2 * P], stack=mid)
            lbt = sb("lbt", [P, 6, 4], stack=mid)
            with ExitStack() as sliding:
                sm = sb("sm", [P, 2, 4, 2 * P], stack=sliding)
                pT = sb("pT", [P, 2, 2, SEQ], stack=sliding)
                smx = sb("smx", [P, 2, 6, 4], stack=sliding)
            ee = sb("ee", [P, 3, SEQ], stack=mid)
            acc = sb("acc", [P, 2, TT, P], stack=mid)
            eb = sb("eb", [P, 3, P], stack=mid)
            kd = sb("kd", [P, 3, P], stack=mid)
            qs = sb("qs", [P, 6, P], stack=mid)
            off = sb("off", [P, 2, 6, P], stack=mid)
        with ExitStack() as late:
            obuf = sb("obuf", [P, 8, SEQ], stack=late)
        a_hi = sb("a_hi", [P, KF, SEQ], F32R)
        a_lo = sb("a_lo", [P, KF, SEQ], F32R)
        cv = sb("cv", [P, 2, SEQ])

        ps = ctx.enter_context(nc.psum_tensor("ps", [P, 8, SEQ], F32))

        s_raw = [sem(f"s_raw{n}") for n in range(2)]
        s_hi = sem("s_hi")
        s_lo = sem("s_lo")
        s_used = sem("s_used")
        s_const = sem("s_const")
        s_cdve = sem("s_cdve")
        s_prow = sem("s_prow")
        s_xin = [sem(f"s_xin{n}") for n in range(2)]
        s_pp = sem("s_pp")
        s_par = sem("s_par")
        s_xp = sem("s_xp")
        s_xT = sem("s_xT")
        s_ss0 = sem("s_ss0")
        s_x = sem("s_x")
        s_sq = sem("s_sq")
        s_stat = sem("s_stat")
        s_var = sem("s_var")
        s_rstd = sem("s_rstd")
        s_diag = sem("s_diag")
        s_rb = sem("s_rb")
        s_ht = sem("s_ht")
        s_hhi = sem("s_hhi")
        s_hlo = sem("s_hlo")
        s_take = sem("s_take")
        s_glu = sem("s_glu")
        s_tap = sem("s_tap")
        s_qsq = sem("s_qsq")
        s_qst = sem("s_qst")
        s_qv = sem("s_qv")
        s_qr = sem("s_qr")
        s_qb = sem("s_qb")
        s_qn = sem("s_qn")
        s_vt = sem("s_vt")
        s_vc = sem("s_vc")
        s_z = sem("s_z")
        s_ab = sem("s_ab")
        s_l = sem("s_l")
        s_sp = sem("s_sp")
        s_spl = sem("s_spl")
        s_tail = sem("s_tail")
        s_dm = sem("s_dm")
        s_w = sem("s_w")
        s_pv = sem("s_pv")
        s_mhi = sem("s_mhi")
        s_mlo = sem("s_mlo")
        s_mean = sem("s_mean")
        s_cen = sem("s_cen")
        s_csq = sem("s_csq")
        s_ly = sem("s_ly")
        s_ls = sem("s_ls")
        s_out = sem("s_out")
        s_t0 = sem("s_t0")
        s_tp = sem("s_tp")
        s_conv = sem("s_conv")
        s_silu = sem("s_silu")
        s_gv = sem("s_gv")
        s_ahi = sem("s_ahi")
        s_alo = sem("s_alo")
        s_sink = sem("s_sink")
        s_take2 = sem("s_take2")
        s_ks = sem("s_ks")
        s_vtp = sem("s_vtp")
        s_vt2 = sem("s_vt2")
        s_gc = sem("s_gc")
        s_lb = sem("s_lb")
        s_sc = sem("s_sc")
        s_sm = sem("s_sm")
        s_mx = sem("s_mx")
        s_pe = sem("s_pe")
        s_den = sem("s_den")
        s_p = sem("s_p")
        s_tr = sem("s_tr")
        s_pT = sem("s_pT")
        s_po = sem("s_po")
        s_ohi = sem("s_ohi")
        s_olo = sem("s_olo")
        s_f = sem("s_f")
        s_lf = sem("s_lf")
        s_b = sem("s_b")
        s_dif = sem("s_dif")
        s_e = sem("s_e")
        s_ek = sem("s_ek")
        s_eq = sem("s_eq")
        s_lv = sem("s_lv")
        s_cp = sem("s_cp")
        s_of = sem("s_of")
        s_ofe = sem("s_ofe")
        s_ofk = sem("s_ofk")
        s_ofp = sem("s_ofp")
        s_ofc = sem("s_ofc")
        s_pvh = sem("s_pvh")
        s_oc = sem("s_oc")
        s_yn = sem("s_yn")
        s_g2 = sem("s_g2")
        s_g2hi = sem("s_g2hi")
        s_g2lo = sem("s_g2lo")
        s_vh = sem("s_vh")
        s_gsil = sem("s_gsil")
        s_gx = sem("s_gx")
        s_ft = sem("s_ft")
        s_fin = sem("s_fin")
        s_st = sem("s_st")

        def halves(t, m):
            return t.rearrange("p (n two m) -> p n two m", two=2, m=m)

        def chunks(t):
            return t.rearrange("p (c n) -> p c n", n=P)

        def zps(h):
            b = 3 * (h % 2)
            return ps[:, b:b + 3, :].rearrange("p b n -> p (b n)")[:, 0:ZW]

        def unit_raw(u, down):
            pair = w_raw[:, (u // 2) % 2, :]
            if down:
                return pair.rearrange("p (c n) -> p c n", c=2)[:, u % 2, :]
            return pair.rearrange("p (k c n) -> p k c n", k=KD, c=2)[:, :, u % 2, :]

        def unit_view(t, u, down):
            w = t[:, u % 4, :]
            return w if down else w.rearrange("p (k n) -> p k n", k=KD)

        def is_down(u):
            return U_DOWN <= u < U_IN2 or U_DOWN2 <= u < U_END

        block = ctx.enter_context(nc.Block())

        @block.sync
        def _(sp):
            def pair(p, src, at=None, first=False):
                slot = p % 2 if at is None else at
                if not first:
                    sp.wait_ge(s_lo, 2 * p - 2)
                sp.dma_start(w_raw[:, slot, :].rearrange("p (k n) -> p k n", n=src.shape[-1]),
                             src).then_inc(s_raw[slot], 16)

            def cols(w, c0):
                return w[0].rearrange("(k p) n -> p k n", p=P)[:, :, bass.ds(c0, 2 * P)]

            def rows(w, k0):
                return w[0].rearrange("(k p) n -> p k n", p=P)[:, bass.ds(k0, 2), :]

            for n in range(2):
                sp.dma_start(xtok[:, 2 * n:2 * n + 2, :],
                             x[0, 2 * n * P:2 * (n + 1) * P, :].rearrange("(t p) d -> p t d", p=P)).then_inc(s_xin[n], 16)
            A0, B0, V0 = 1536, 2048, 1024
            in_cols = [B0, A0, B0 + 256, A0 + 256, 0, 256, 512, 768, V0, V0 + 256]
            for n, c0 in enumerate(in_cols):
                pair(n, cols(w_in, c0), first=n < 2)
            for n in range(4):
                pair(U_OUT // 2 + n, cols(w_out, 256 * n))

            def up(gate, val, v0, u0):
                with sp.Fori(0, NUP) as i:
                    pair(u0 // 2 + 2 * i, cols(gate, 256 * i), at=(u0 // 2) % 2)
                    pair(u0 // 2 + 1 + 2 * i, cols(val, v0 + 256 * i), at=(u0 // 2 + 1) % 2)

            def down(w, u0):
                pair(u0 // 2, rows(w, 0))
                with sp.Fori(0, 5) as i:
                    pair(u0 // 2 + 1 + 2 * i, rows(w, 4 * i + 2), at=(u0 // 2 + 1) % 2)
                    pair(u0 // 2 + 2 + 2 * i, rows(w, 4 * i + 4), at=(u0 // 2) % 2)

            up(w_up, w_up, DFF, U_UP)
            down(w_down, U_DOWN)
            for n, c0 in enumerate((2560, 2048, 2304, 512, 768, 0, 256, 1024, 1280, 1536, 1792)):
                pair(U_IN2 // 2 + n, cols(w_in_2, c0))
            for n in range(4):
                pair(U_OUT2 // 2 + n, cols(w_out_2, 256 * n))
            up(w_gate_2, w_up_2, 0, U_UP2)
            down(w_down_2, U_DOWN2)
            for done, n in enumerate(OUT_ORDER):
                t, half = n // 2, n % 2
                sp.wait_ge(s_fin, done + 1)
                sp.dma_start(out[0, t * P:(t + 1) * P, 512 * half:512 * (half + 1)],
                             obuf[:, n, :]).then_inc(s_st, 16)
            sp.wait_ge(s_st, 16 * 8)

        @block.gpsimd
        def _(pool):
            pool.memset(ident[:], 0.0).then_inc(s_const, 1)
            pool.memset(ones[:], 1.0).then_inc(s_const, 1)
            pool.memset(mhalf[:], -0.5).then_inc(s_const, 1)
            pool.wait_ge(s_const, 3)
            pool.affine_select(out=ident[:], in_=ident[:], compare_op=ALU.not_equal, fill=1.0, base=0,
                               pattern=[[-1, P]], channel_multiplier=1).then_inc(s_const, 1)
            pool.memset(sel[:], 1.0).then_inc(s_const, 1)
            pool.memset(selT[:], 1.0).then_inc(s_const, 1)
            pool.memset(lnone[:], 1.0 / (CT * P)).then_inc(s_const, 1)
            pool.memset(smask[:], 1.0).then_inc(s_const, 1)
            pool.memset(nmask[:], 0.0).then_inc(s_const, 1)
            pool.memset(ntri_f[:], -1.0).then_inc(s_const, 1)
            pool.memset(glu[:, :, 0:PAD], 0.0).then_inc(s_const, 1)
            pool.wait_ge(s_const, 11)
            pool.affine_select(out=sel[:], in_=sel[:], compare_op=ALU.is_ge, fill=0.0, base=0,
                               pattern=[[P, 8], [-64, 16]], channel_multiplier=1).then_inc(s_const, 1)
            pool.affine_select(out=selT[:], in_=selT[:], compare_op=ALU.is_ge, fill=0.0, base=0,
                               pattern=[[P, 8], [1, P]], channel_multiplier=-64).then_inc(s_const, 1)
            pool.affine_select(out=smask[:], in_=smask[:], compare_op=ALU.is_gt, fill=0.0, base=0,
                               pattern=[[1, P]], channel_multiplier=-1).then_inc(s_const, 1)
            pool.affine_select(out=nmask[:], in_=nmask[:], compare_op=ALU.is_gt, fill=NEG, base=0,
                               pattern=[[1, P]], channel_multiplier=-1).then_inc(s_const, 1)
            pool.affine_select(out=ntri_f[:], in_=ntri_f[:], compare_op=ALU.is_ge, fill=0.0, base=0,
                               pattern=[[-1, P]], channel_multiplier=1).then_inc(s_const, 1)
            pool.wait_ge(s_const, 16)
            pool.affine_select(out=sel[:], in_=sel[:], compare_op=ALU.is_ge, fill=0.0, base=63,
                               pattern=[[-P, 8], [64, 16]], channel_multiplier=-1).then_inc(s_const, 1)
            pool.affine_select(out=selT[:], in_=selT[:], compare_op=ALU.is_ge, fill=0.0, base=63,
                               pattern=[[-P, 8], [-1, P]], channel_multiplier=64).then_inc(s_const, 1)

            def rest(at, i=0):
                pool.wait_ge(s_hi, at + 4 * i + 1)
                down = is_down(at)
                pool.tensor_tensor(unit_view(w_lo, at, down), unit_raw(at, down),
                                   unit_view(w_hi, at, down).bitcast(F32), ALU.subtract).then_inc(s_lo, 1)

            def rests(u0, n):
                if n >= 8:
                    with pool.Fori(0, n // 4) as i:
                        for c in range(4):
                            rest(u0 + c, i)
                    u0, n = u0 + 4 * (n // 4), n % 4
                for c in range(n):
                    rest(u0 + c)

            def inverse_root(n):
                pool.wait_ge(s_var, n)
                pool.tensor_tensor(rstd[:], stat[:], mhalf[:], ALU.pow).then_inc(s_rstd, 1)

            inverse_root(1)
            rests(U_IN, 20)
            rests(U_OUT, 4)
            inverse_root(2)
            rests(U_OUT + 4, 4)
            rests(U_UP, 3)
            inverse_root(3)
            rests(U_UP + 3, 1)
            rests(U_UP + 4, 40)
            rests(U_DOWN, 22)
            rests(U_IN2, 2)
            inverse_root(4)
            rests(U_IN2 + 2, 4)
            pool.wait_ge(s_used, U_IN2)
            steps = [s_gc, 0]
            def link(ins):
                steps[1] += 1
                ins.then_inc(s_gc, 1)
                pool.wait_ge(s_gc, steps[1])
            link(pool.memset(lmask[:], 0))
            for lv in range(7):
                m = 1 << lv
                upper = lmask[:, lv, :].rearrange("p (n two m) -> p n two m", two=2, m=m)[:, :, 1, :]
                n = P // (2 * m)
                link(pool.memset(upper, 1))
                link(pool.affine_select(out=upper, in_=upper, compare_op=ALU.is_ge, fill=0, base=0,
                                        pattern=[[-2 * m, n], [0, m]], channel_multiplier=1))
                link(pool.affine_select(out=upper, in_=upper, compare_op=ALU.is_ge, fill=0, base=m - 1,
                                        pattern=[[2 * m, n], [0, m]], channel_multiplier=-1))
            link(pool.memset(cmask[:], 1.0))
            link(pool.memset(cmask[:, 0:SEQ:P], 0.0))
            link(pool.memset(band[:], 0.0))
            link(pool.affine_select(out=band[:, 0:P], in_=band[:, 0:P], compare_op=ALU.is_gt, fill=NEG, base=0,
                                    pattern=[[1, P]], channel_multiplier=-1))
            link(pool.affine_select(out=band[:, P:], in_=band[:, P:], compare_op=ALU.is_ge, fill=NEG, base=0,
                                    pattern=[[-1, P]], channel_multiplier=1))
            assert steps[1] == GC
            rests(U_IN2 + 6, 12)

            def times_queries(i):
                j, m = i // 8, 1 << (i % 8 - 1)
                pool.wait_ge(s_e, 7 * j + i % 8)
                up = halves(ee[:, i % 3, :], m)[:, :, 1, :]
                pool.tensor_tensor(up, up, halves(qq[:, j, :], m)[:, :, 1, :], ALU.mult).then_inc(s_eq, 1)

            for i in range(32):
                if i % 8:
                    times_queries(i)
                if i == 8:
                    rests(U_IN2 + 18, 4)
                if i > 8 and i % 8 == 5:
                    inverse_root(4 + i // 8)
                if i - 1 in FILL[4:]:
                    rests(U_OUT2 + FILL[4:].index(i - 1), 1)
            inverse_root(8)
            rests(U_OUT2 + 4, 4)
            rests(U_UP2, 3)
            inverse_root(9)
            rests(U_UP2 + 3, 1)
            rests(U_UP2 + 4, 40)
            rests(U_DOWN2, 22)
            inverse_root(10)

        @block.scalar
        def _(act):
            def row(t, r0, src, c0=0):
                act.dma_start(prow[r0:r0 + src.shape[0], t, c0:c0 + src.shape[1]], src).then_inc(s_prow, 16)
            for r0, a in ((C_N1, norm1_g), (C_N2, norm2_g), (C_NM, norm_mix_w_2), (C_NF, norm_ffn_w_2),
                          (C_CB, conv_dw_b), (C_LG, conv_ln_g), (C_LB, conv_ln_b), (C_LL, lb_logits_2),
                          (C_HG, hg_norm_w_2), (C_FB, ffn_dw_b), (C_FB2, conv_b_2), (C_BA, b_attn_2),
                          (C_FN, final_norm_w_2.rearrange("(l n) -> l n", l=1))):
                row(0, r0, a.rearrange("l (c p) -> (l c) p", p=P))
            for r0, a in ((C_QG, q_norm_g), (C_KG, k_norm_g)):
                row(0, r0, a, 0)
                row(0, r0, a, 64)
            for t, a in ((1, ffn_dw_w), (2, conv_w_2), (3, conv_dw_w)):
                row(t, 0, a.rearrange("l k (c p) -> (l k c) p", p=P))

            act.dma_start(sinkb[:], sinks_2.to_broadcast([P, 8])).then_inc(s_sink, 16)

            def table(n):
                act.add_instruction(mybir.InstLoadActFuncSet(name=nc.get_next_instruction_name(),
                                                             act_func_set_id=n, ins=[], outs=[]))

            def lead(at, i=0):
                act.wait_ge(s_raw[(at // 2) % 2], 16 * (at // 4 + 1) + 16 * i)
                if at >= 4:
                    act.wait_ge(s_used, at + 4 * i - 3)
                down = is_down(at)
                act.activation(unit_view(w_hi, at, down), unit_raw(at, down), ACT.Copy).then_inc(s_hi, 1)

            for t in range(TT):
                act.wait_ge(s_xin[t // 2], 16)
                if t:
                    act.wait_ge(s_ss0, t)
                act.activation(xjunk[:], xtok[:, t, :], ACT.Square, accum_out=ss0[:, t:t + 1]).then_inc(s_ss0, 1)
            for m in range(KD):
                act.wait_ge(s_xp, m + 1)
                act.activation(xT[:, m, :], ps[:, 4 + m % 4, :], ACT.Copy).then_inc(s_xT, 1)
            for u in range(4):
                lead(u)

            def norm_hi(n):
                for k in range(KD):
                    act.wait_ge(s_ht, KD * n + k + 1)
                    act.activation(h_hi[:, k, :], htmp[:, k % 2, :], ACT.Copy).then_inc(s_hhi, 1)

            norm_hi(0)
            for i in range(2):
                for c in range(4):
                    u = 4 * i + c
                    act.wait_ge(s_used, u + 1)
                    if c < 2:
                        act.activation(cy[:, 2 * i + c, :], ps[:, c, :], ACT.Sigmoid).then_inc(s_take, 1)
                    else:
                        act.activation(glu[:, 2 * i + c - 2, PAD:PAD + SEQ], ps[:, c, :], ACT.Copy).then_inc(s_take, 1)
                    lead(u + 4)
            act.wait_ge(s_par, 4)
            act.wait_ge(s_ss0, TT)
            for u in range(8, 16):
                act.wait_ge(s_used, u + 1)
                act.activation(qk[:, u - 8, :], ps[:, u % 4, :], ACT.Copy).then_inc(s_take, 1)
                lead(u + 4)
                act.wait_ge(s_take, u + 1)
                act.activation(sqk[:, u - 8, :], qk[:, u - 8, :], ACT.Square).then_inc(s_qsq, 1)
            def value(t):
                if t < TT - 1:
                    act.wait_ge(s_vt, t + 1)
                else:
                    act.wait_ge(s_used, 20)
                act.activation(vtok[:, t, :], ps[:, t, :], ACT.Copy).then_inc(s_vc, 1)
            value(0)
            value(1)
            table(6)
            act.wait_ge(s_qv, 1)
            act.activation(nvar[:, 1, :], nvar[:, 0, :], ACT.Ln).then_inc(s_qr, 1)
            act.wait_ge(s_qr, 1)
            act.activation(nvar[:, 1, :], nvar[:, 1, :], ACT.Exp, scale=-0.5).then_inc(s_qr, 1)
            value(2)
            value(3)
            for u in range(U_OUT, U_OUT + 4):
                lead(u)

            ln_sq = [sq[:, 0, :], sq[:, 1, :], htmp[:, 0, :], htmp[:, 1, :]]
            for s in range(AH + 3):
                if s >= 3 and (s - 3) % 2 == 1:
                    j = (s - 3) // 2
                    act.wait_ge(s_pv, 2 * j + 2)
                    act.activation(h_hi[:, j, :], ps[:, 6, :], ACT.Copy).then_inc(s_mhi, 1)
                if s < AH:
                    z = zl[:, s % 3, :]
                    act.wait_ge(s_z, s + 1)
                    if s >= 3:
                        act.wait_ge(s_pv, s - 2)
                    act.activation(z, zps(s), ACT.Abs).then_inc(s_ab, 1)
                    act.wait_ge(s_ab, 2 * s + 1)
                    act.activation(z, z, ACT.Exp, scale=-1.0).then_inc(s_ab, 1)
                    act.wait_ge(s_ab, 2 * s + 2)
                    act.activation(z, z, ACT.Ln, bias=1.0).then_inc(s_l, 1)
                if 1 <= s <= AH:
                    act.wait_ge(s_dm, 2 * s)
                    act.activation(zl[:, (s - 1) % 3, :], zps(s - 1), ACT.Exp).then_inc(s_w, 1)
                if s == 2:
                    for c in range(CT):
                        act.wait_ge(s_cen, c + 1)
                        act.activation(ln_sq[c], cy[:, c, :], ACT.Square).then_inc(s_csq, 1)
                if s == 7:
                    for c in range(CT):
                        act.wait_ge(s_ly, c + 1)
                        act.activation(cy[:, c, :], cy[:, c, :], ACT.Silu, bias=par[:, 0, C_LB + c:C_LB + c + 1]).then_inc(s_ls, 1)
                    for c in range(CT):
                        act.wait_ge(s_ls, c + 1)
                        act.activation(h_hi[:, CT + c, :], cy[:, c, :], ACT.Copy).then_inc(s_mhi, 1)
                    table(6)

            def squares(n, m):
                act.wait_ge(s_x, 8 * (n - 1) + m + 1)
                act.wait_ge(s_stat, STATS[n] + max(m - 1, 0))
                act.activation(sq[:, m % 2, :], xT[:, m, :], ACT.Square).then_inc(s_sq, 1)

            for m in range(KD):
                squares(1, m)
                lead(U_OUT + 4 + m)
            norm_hi(1)

            def ffn(lay, u0, wcol, bcol):
                def quad(i, leads, wait=True):
                    j0 = KF * lay + 2 * i
                    def tap0(c):
                        act.activation(cv[:, c, :], ps[:, c, :], ACT.Identity,
                                       scale=par[:, 1 + lay, bass.ds(2 * KF + 2 * i + c, 1)],
                                       bias=par[:, 0, bass.ds(bcol + 2 * i + c, 1)]).then_inc(s_t0, 1)
                    def silu(c):
                        act.wait_ge(s_conv, j0 + c + 1)
                        act.activation(cv[:, c, :], cv[:, c, :], ACT.Silu).then_inc(s_silu, 1)
                    def hi(c):
                        act.wait_ge(s_gv, j0 + c + 1)
                        act.activation(a_hi[:, bass.ds(2 * i + c, 1), :].rearrange("p a n -> p (a n)"),
                                       cv[:, c, :], ACT.Copy).then_inc(s_ahi, 1)
                    for c in range(4):
                        act.wait_ge(s_used, u0 + 4 * i + c + 1)
                        if c < 2:
                            if wait:
                                act.wait_ge(s_alo, j0 + c - 1)
                            tap0(c)
                        leads(c)
                        if c >= 1 and c < 3:
                            silu(c - 1)
                        if c == 3:
                            hi(0)
                    hi(1)
                quad(0, lambda c: lead(u0 + 4 + c), wait=lay > 0)
                with act.Fori(1, NUP - 1) as i:
                    quad(i, lambda c: lead(u0 + 4 + c, i))
                quad(NUP - 1, lambda c: lead(u0 + 4 * NUP + c))

            def down(n, u0, more):
                with act.Fori(0, 4) as i:
                    for c in range(4):
                        act.wait_ge(s_used, u0 + 4 * i + c + 1)
                        lead(u0 + 4 + c, i)
                for c in range(16, KF - 1):
                    if c < KF - 4 or more:
                        lead(u0 + c + 4)
                for m in range(KD):
                    squares(n, m)
                    if m == KD - 2 and more:
                        lead(u0 + KF + 3)

            ffn(0, U_UP, 1, C_FB)
            down(2, U_DOWN, True)
            norm_hi(2)

            def bias(c):
                return par[:, 0, C_BA + c:C_BA + c + 1]

            def take(n, out_ap, in_ap, func=ACT.Copy, **kw):
                act.wait_ge(s_used, U_IN2 + n + 1)
                act.activation(out_ap, in_ap, func, **kw).then_inc(s_take2, 1)

            take(0, kT[:, 0, :], ps[:, 2, :], ACT.Identity, bias=bias(4))
            take(1, vT[:], ps[:, 3, :], ACT.Identity, bias=bias(5))
            act.wait_ge(s_take2, 1)
            for half in range(2):
                act.dma_start(kT[64 * half:64 * half + 64, 1, :],
                              kT[64 - 64 * half:128 - 64 * half, 0, :]).then_inc(s_ks, 16)
            lead(U_IN2 + 4)
            lead(U_IN2 + 5)
            for c in range(4):
                take(2 + c, aq[:, c, :], ps[:, c, :], ACT.Identity, bias=bias(c))
                lead(U_IN2 + 6 + c)
                if c == 1:
                    act.wait_ge(s_vtp, 1)
                    act.activation(vt2[:].rearrange("p t n -> p (t n)"), ps[:, 6, :], ACT.Copy).then_inc(s_vt2, 1)
            table(6)
            act.wait_ge(s_lb, 3)
            act.activation(lbt[:, 1:3, :], lbt[:, 1:3, :], ACT.Exp).then_inc(s_lb, 1)

            def o_hi(n):
                b, g = n // 2, n % 2
                act.wait_ge(s_po, n + 1)
                act.activation(m_hi[:, 2 * g:2 * g + 2, b * P:(b + 1) * P],
                               ps[:, 6, 0:2 * P].rearrange("p (j q) -> p j q", j=2), ACT.Copy).then_inc(s_ohi, 1)

            for n in range(8):
                p, w = sm[:, n % 2], smx[:, n % 2]
                lo = P if n < 2 else 0
                act.wait_ge(s_mx, 4 * n + 4)
                for a in range(4):
                    act.activation(p[:, a, lo:], p[:, a, lo:], ACT.Exp, bias=w[:, 1, a:a + 1],
                                   accum_out=w[:, 3, a:a + 1]).then_inc(s_pe, 1)
                act.activation(w[:, 2, :], w[:, 2, :], ACT.Exp).then_inc(s_pe, 1)
                if n >= 1:
                    o_hi(n - 1)
                if n < 4:
                    take(6 + n, kk[:, n, :], ps[:, n, :])
                else:
                    take(6 + n, qq[:, n - 4, :], ps[:, n - 4, :], scale=float(P) ** -0.5)
                lead(U_IN2 + 10 + n)
                for half in range(1 if n < 2 else 0, 2):
                    act.wait_ge(s_tr, n + 1)
                    if n >= 2:
                        act.wait_ge(s_po, n - 1)
                    act.activation(pT[:, n % 2, half, :], ps[:, 6 + half, :], ACT.Copy).then_inc(s_pT, 1)
                if n == 5:
                    act.wait_ge(s_take2, 10)
                    for j in range(4):
                        act.activation(kk[:, j, :], kk[:, j, :], ACT.Sigmoid).then_inc(s_lf, 1)
                    table(6)
            o_hi(7)
            for j in range(4):
                act.wait_ge(s_f, 2 * j + 2)
                act.activation(bb[:, j, :], bb[:, j, :], ACT.Ln).then_inc(s_lf, 1)

            def between(j):
                act.wait_ge(s_of, j + 1)
                act.activation(kd[:], kd[:], ACT.Exp).then_inc(s_ofe, 1)
                act.activation(eb[:], chunks(bb[:, j, :])[:, 1:4, :], ACT.Exp).then_inc(s_ofe, 1)

            def after(i):
                j, lv = i // 8, i % 8
                if lv == 2:
                    act.wait_ge(s_pvh, j + 1)
                    if j >= 2:
                        act.wait_ge(s_yn, j - 1)
                    act.activation(htmp[:, j % 2, :], ps[:, 6, :], ACT.Copy).then_inc(s_oc, 1)
                    act.wait_ge(s_oc, 2 * j + 1)
                    act.activation(sq[:, j % 2, :], htmp[:, j % 2, :], ACT.Square).then_inc(s_oc, 1)

            def copy_between(j):
                act.wait_ge(s_ofp, j + 1)
                if j >= 2:
                    act.wait_ge(s_pvh, j - 1)
                act.activation(off[:, j % 2, 0:4, :].rearrange("p c n -> p (c n)"), ps[:, 6, :], ACT.Copy).then_inc(s_ofc, 1)
                act.activation(off[:, j % 2, 4:6, :].rearrange("p c n -> p (c n)"), ps[:, 7, 0:2 * P], ACT.Copy).then_inc(s_ofc, 1)

            for i in range(32):
                j, lv = i // 8, i % 8
                if lv == 0:
                    between(j)
                if lv:
                    act.wait_ge(s_dif, 7 * j + lv)
                    act.activation(ee[:, i % 3, :], ee[:, i % 3, :], ACT.Exp).then_inc(s_e, 1)
                if lv == 0 and j:
                    copy_between(j - 1)
                if j:
                    after(i - 8)
                if i in FILL:
                    t = FILL.index(i)
                    if t < 3:
                        act.wait_ge(s_vh, t + 1)
                        act.activation(vh[:, t, :], ps[:, t, :], ACT.Copy).then_inc(s_take2, 1)
                    elif t == 3:
                        act.wait_ge(s_used, U_IN2 + 18)
                        act.activation(vh[:, t, :], ps[:, t, :], ACT.Copy).then_inc(s_take2, 1)
                        for c in range(4):
                            lead(U_IN2 + 18 + c)
                    else:
                        take(14 + t, aq[:, t - 4, :], ps[:, t - 4, :])
                        lead(U_OUT2 + t - 4)
            copy_between(3)
            after(26)
            act.wait_ge(s_take2, 22)
            for j in range(4):
                act.activation(aq[:, j, :], aq[:, j, :], ACT.Silu).then_inc(s_gsil, 1)
            for j in range(4):
                act.wait_ge(s_g2, j + 1)
                act.activation(h_hi[:, j, :], kk[:, j, :], ACT.Copy).then_inc(s_g2hi, 1)

            for m in range(KD):
                squares(3, m)
                lead(U_OUT2 + 4 + m)
            norm_hi(3)
            ffn(1, U_UP2, 2, C_FB2)
            down(4, U_DOWN2, False)
            act.wait_ge(s_sq, 8 * 4)
            for m in range(KD):
                act.activation(xT[:, m, :], xT[:, m, :], ACT.Copy, scale=par[:, 0, C_FN + m:C_FN + m + 1]).then_inc(s_gx, 1)

        @block.vector
        def _(dve):
            counts = {}
            def link(ins, s, base=0):
                counts[s] = counts.get(s, base) + 1
                ins.then_inc(s, 1)
                dve.wait_ge(s, counts[s])

            dve.wait_ge(s_const, 16)
            dve.tensor_copy(ntri[:], ntri_f[:]).then_inc(s_cdve, 1)
            dve.tensor_scalar(nones[:], ones[:], -1.0, None, ALU.mult).then_inc(s_cdve, 1)
            for t, n in enumerate(PROWS):
                dve.wait_ge(s_pp, t + 1)
                dve.tensor_copy(par[:, t, 0:n], ps[:, t, 0:n]).then_inc(s_par, 1)
            dve.wait_ge(s_par, 4)
            dve.tensor_scalar(gq8[:], par[:, 0, C_QG:C_QG + 1], 0.125, None, ALU.mult).then_inc(s_cdve, 1)

            def spread(n):
                dve.wait_ge(s_rstd, n)
                dve.tensor_tensor(diag[:], ident[:, None, :].to_broadcast([P, TT, P]),
                                  rstd[:, :, None].to_broadcast([P, TT, P]), ALU.mult).then_inc(s_diag, 1)

            def variance(src, div, lap):
                dve.tensor_scalar(stat[:], src, 1.0 / div, EPS, ALU.mult, ALU.add).then_inc(s_var, 1)

            def normalize(n, rb_n, gcol, bank):
                def rest(k):
                    dve.wait_ge(s_hhi, KD * n + k + 1)
                    dve.tensor_tensor(h_lo[:, k, :], htmp[:, k % 2, :], h_hi[:, k, :].bitcast(F32),
                                      ALU.subtract).then_inc(s_hlo, 1)
                dve.wait_ge(s_rb, rb_n)
                for k in range(KD):
                    if k >= 2:
                        dve.wait_ge(s_hlo, KD * n + k - 1)
                    dve.scalar_tensor_tensor(htmp[:, k % 2, :], xT[:, k, :], par[:, 0, gcol + k:gcol + k + 1],
                                             ps[:, bank, :], ALU.mult, ALU.mult).then_inc(s_ht, 1)
                    if k >= 1:
                        rest(k - 1)
                rest(KD - 1)

            dve.wait_ge(s_ss0, TT)
            variance(ss0[:], DM, 0)
            spread(1)
            dve.wait_ge(s_xT, KD)
            normalize(0, 1, C_N1, 5)

            for i in range(2):
                dve.wait_ge(s_take, 8 * i // 2 + 4)
                for c in range(2):
                    j = 2 * i + c
                    dve.tensor_tensor(glu[:, j, PAD:PAD + SEQ], glu[:, j, PAD:PAD + SEQ], cy[:, j, :],
                                      ALU.mult).then_inc(s_glu, 1)
                dve.wait_ge(s_glu, 2 * i + 2)
                t0 = 2 * CK * i
                for c in range(2):
                    j = 2 * i + c
                    dve.tensor_scalar(cy[:, j, :], glu[:, j, 0:SEQ], par[:, 3, j:j + 1],
                                      par[:, 0, C_CB + j:C_CB + j + 1], ALU.mult, ALU.add).then_inc(s_tap, 1)
                with dve.Fori(0, PAD // 5) as n:
                    for r in range(5):
                        for c in range(2):
                            j = 2 * i + c
                            dve.wait_ge(s_tap, t0 + 10 * n + 2 * r + c + 1)
                            dve.scalar_tensor_tensor(
                                cy[:, j, :], glu[:, j, bass.ds(5 * n + r + 1, SEQ)],
                                par[:, 3, bass.ds(20 * n + 4 * r + 4 + j, 1)], cy[:, j, :],
                                ALU.mult, ALU.add).then_inc(s_tap, 1)

            dve.wait_ge(s_qst, 1)
            link(dve.tensor_scalar(nvar[:, 0, :], ps[0:16, 4, :], 1.0 / 64, EPS, ALU.mult, ALU.add), s_qv)
            dve.wait_ge(s_qr, 2)
            link(dve.tensor_tensor(nvar[:, 2, :], nvar[:, 1, :], nvar[:, 1, :], ALU.mult), s_qv)
            link(dve.tensor_tensor(nvar[:, 2, :], nvar[:, 2, :], nvar[:, 0, :], ALU.mult), s_qv)
            link(dve.tensor_scalar(nvar[:, 2, :], nvar[:, 2, :], -0.5, 1.5, ALU.mult, ALU.add), s_qv)
            link(dve.tensor_tensor(nvar[:, 1, :], nvar[:, 1, :], nvar[:, 2, :], ALU.mult), s_qv)
            dve.wait_ge(s_cdve, 3)
            for j in range(8):
                g = gq8[:, 0:1] if j < 4 else par[:, 0, C_KG:C_KG + 1]
                dve.wait_ge(s_qb, j + 1)
                dve.scalar_tensor_tensor(qk[:, j, :], qk[:, j, :], g, ps[:, 4 + j % 4, :],
                                         ALU.mult, ALU.mult).then_inc(s_qn, 1)

            def blocks(t):
                return t.rearrange("p (a n) -> p a n", n=P)[:, 0:9:4, :], t[:, ZOFF[1]:ZOFF[1] + P]

            for s in range(AH + 3):
                if s >= 3 and (s - 3) % 2 == 1:
                    j = (s - 3) // 2
                    dve.wait_ge(s_mhi, j + 1 + (CT if j >= 2 else 0))
                    dve.tensor_tensor(h_lo[:, j, :], ps[:, 6, :], h_hi[:, j, :].bitcast(F32),
                                      ALU.subtract).then_inc(s_mlo, 1)
                if 1 <= s <= AH:
                    dve.wait_ge(s_tail, s)
                    three, one = blocks(zps(s - 1))
                    dve.scalar_tensor_tensor(three, three, 0.0, nmask[:, None, :].to_broadcast([P, 3, P]),
                                             ALU.min, ALU.add).then_inc(s_dm, 1)
                    dve.scalar_tensor_tensor(one, one, 0.0, nmask[:], ALU.min, ALU.add).then_inc(s_dm, 1)
                if s == 2:
                    dve.wait_ge(s_mean, 1)
                    for c in range(CT):
                        dve.tensor_tensor(cy[:, c, :], cy[:, c, :], ps[:, 7, :], ALU.subtract).then_inc(s_cen, 1)
                if s == 4:
                    dve.wait_ge(s_stat, CT)
                    variance(ps[:, 7, 0:TT], CT * P, 1)
                    spread(2)
                if s == 6:
                    dve.wait_ge(s_rb, 2)
                    for c in range(CT):
                        dve.scalar_tensor_tensor(cy[:, c, :], cy[:, c, :], par[:, 0, C_LG + c:C_LG + c + 1],
                                                 ps[:, 7, :], ALU.mult, ALU.mult).then_inc(s_ly, 1)
                if s < AH:
                    z = zl[:, s % 3, :]
                    dve.wait_ge(s_l, s + 1)
                    link(dve.scalar_tensor_tensor(z, zps(s), 0.0, z, ALU.max, ALU.add), s_sp)
                    three, one = blocks(z)
                    dve.tensor_tensor(three, three, smask[:, None, :].to_broadcast([P, 3, P]), ALU.mult).then_inc(s_sp, 1)
                    counts[s_sp] += 1
                    link(dve.tensor_tensor(one, one, smask[:], ALU.mult), s_sp)
                    if s >= 2:
                        dve.wait_ge(s_tail, s - 1)
                    link(dve.tensor_copy(sp_hi[:, s % 2, :], z), s_sp)
                    dve.tensor_tensor(sp_lo[:, s % 2, :], z, sp_hi[:, s % 2, :].bitcast(F32),
                                      ALU.subtract).then_inc(s_spl, 1)
                if s == 9:
                    for c in range(CT):
                        dve.wait_ge(s_mhi, 2 + c + 1)
                        dve.tensor_tensor(h_lo[:, CT + c, :], cy[:, c, :], h_hi[:, CT + c, :].bitcast(F32),
                                          ALU.subtract).then_inc(s_mlo, 1)

            def residual(m, bank, sem, value):
                dve.wait_ge(sem, value)
                dve.tensor_tensor(xT[:, m, :], xT[:, m, :], ps[:, bank, :], ALU.add).then_inc(s_x, 1)

            def norm(n, stats, rb_n, gcol):
                dve.wait_ge(s_stat, stats)
                variance(ps[:, 4, 0:TT], DM, n)
                if gcol is not None:
                    spread(rb_n)
                    normalize(n, rb_n, gcol, 5)

            for m in range(KD):
                residual(m, m % 4, s_used, U_OUT + m + 1)
            norm(1, CT + 8, 3, C_N2)

            def ffn(lay):
                def quad(i):
                    j0 = KF * lay + 2 * i
                    for c in range(2):
                        w = 1 + lay
                        dve.wait_ge(s_t0, j0 + c + 1)
                        dve.scalar_tensor_tensor(cv[:, c, 1:], ps[:, c, 0:SEQ - 1],
                                                 par[:, w, bass.ds(KF + 2 * i + c, 1)], cv[:, c, 1:],
                                                 ALU.mult, ALU.add).then_inc(s_tp, 1)
                        dve.wait_ge(s_tp, j0 + c + 1)
                        dve.scalar_tensor_tensor(cv[:, c, 2:], ps[:, c, 0:SEQ - 2],
                                                 par[:, w, bass.ds(2 * i + c, 1)], cv[:, c, 2:],
                                                 ALU.mult, ALU.add).then_inc(s_conv, 1)
                    for c in range(2):
                        dve.wait_ge(s_silu, j0 + c + 1)
                        dve.wait_ge(s_used, (U_UP2 if lay else U_UP) + 4 * i + 3 + c)
                        dve.tensor_tensor(cv[:, c, :], cv[:, c, :], ps[:, 2 + c, :], ALU.mult).then_inc(s_gv, 1)
                    for c in range(2):
                        dve.wait_ge(s_ahi, j0 + c + 1)
                        dve.tensor_tensor(a_lo[:, bass.ds(2 * i + c, 1), :].rearrange("p a n -> p (a n)"),
                                          cv[:, c, :],
                                          a_hi[:, bass.ds(2 * i + c, 1), :].rearrange("p a n -> p (a n)").bitcast(F32),
                                          ALU.subtract).then_inc(s_alo, 1)
                with dve.Fori(0, NUP) as i:
                    quad(i)

            def down(lay, end):
                for m in range(KD - 1):
                    residual(m, (m + 4) % 8, s_out, (KD - 1) * lay + m + 1)
                residual(KD - 1, 3, s_used, end)

            ffn(0)
            down(0, U_IN2)
            norm(2, STATS[2] + 8, 4, C_NM)

            l0, l1 = (par[:, 0, C_LL + 4 * r:C_LL + 4 * r + 4] for r in range(2))
            dve.wait_ge(s_par, 1)
            link(dve.tensor_tensor(lbt[:, 0, :], l0, l1, ALU.max), s_lb)
            link(dve.tensor_tensor(lbt[:, 1, :], l0, lbt[:, 0, :], ALU.subtract), s_lb)
            link(dve.tensor_tensor(lbt[:, 2, :], l1, lbt[:, 0, :], ALU.subtract), s_lb)
            dve.wait_ge(s_lb, 4)
            counts[s_lb] = 4
            link(dve.tensor_tensor(lbt[:, 0, :], lbt[:, 1, :], lbt[:, 2, :], ALU.add), s_lb)
            link(dve.reciprocal(lbt[:, 0, :], lbt[:, 0, :]), s_lb)
            link(dve.tensor_tensor(lbt[:, 3, :], lbt[:, 1, :], lbt[:, 0, :], ALU.mult), s_lb)
            link(dve.tensor_scalar(lbt[:, 4, :], lbt[:, 3, :], -1.0, 1.0, ALU.mult, ALU.add), s_lb)

            def o_lo(n):
                b, g = n // 2, n % 2
                dve.wait_ge(s_ohi, n + 1)
                dve.tensor_tensor(m_lo[:, 2 * g:2 * g + 2, b * P:(b + 1) * P],
                                  ps[:, 6, 0:2 * P].rearrange("p (j q) -> p j q", j=2),
                                  m_hi[:, 2 * g:2 * g + 2, b * P:(b + 1) * P].bitcast(F32),
                                  ALU.subtract).then_inc(s_olo, 1)

            def pairs(t):
                return t.rearrange("p (h j) -> p h j", h=2)

            dve.wait_ge(s_gc, GC)
            dve.wait_ge(s_sink, 16)
            for n in range(8):
                g = n % 2
                p, w = sm[:, n % 2], smx[:, n % 2]
                lo = P if n < 2 else 0
                dve.wait_ge(s_sc, n + 1)
                if n >= 2:
                    dve.wait_ge(s_tr, n - 1)
                src = ps[:, 4:6, :].rearrange("p b (a k) -> p (b a) k", k=2 * P)
                sink = sinkb[:, 4 * g:4 * g + 4].rearrange("p (j h) -> p h j", h=2)
                dve.scalar_tensor_tensor(p[:, :, lo:], src[:, :, lo:], 0.125,
                                         band[:, None, lo:].to_broadcast([P, 4, 2 * P - lo]),
                                         ALU.mult, ALU.add).then_inc(s_sm, 1)
                dve.wait_ge(s_sm, n + 1)
                link(dve.tensor_reduce(w[:, 0, :], p[:, :, lo:], AX.X, ALU.max), s_mx)
                link(dve.tensor_tensor(pairs(w[:, 0, :]), pairs(w[:, 0, :]), sink, ALU.max), s_mx)
                dve.tensor_scalar(w[:, 1, :], w[:, 0, :], -1.0, None, ALU.mult).then_inc(s_mx, 1)
                counts[s_mx] += 1
                link(dve.tensor_tensor(pairs(w[:, 2, :]), sink, pairs(w[:, 0, :]), ALU.subtract), s_mx)
                if n >= 1:
                    o_lo(n - 1)
                dve.wait_ge(s_pe, 5 * n + 5)
                link(dve.tensor_tensor(w[:, 4, :], w[:, 3, :], w[:, 2, :], ALU.add), s_den)
                link(dve.reciprocal(w[:, 5, :], w[:, 4, :]), s_den)
                dve.tensor_tensor(p[:, :, lo:], p[:, :, lo:],
                                  w[:, 5, :, None].to_broadcast([P, 4, 2 * P - lo]), ALU.mult).then_inc(s_p, 1)
            for j in range(4):
                dve.wait_ge(s_lf, j + 1)
                link(dve.tensor_scalar(bb[:, j, :], kk[:, j, :], lbt[:, 4, j:j + 1], lbt[:, 3, j:j + 1],
                                       ALU.mult, ALU.add), s_f)
                dve.tensor_scalar(kk[:, j, :], bb[:, j, :], -1.0, 1.0, ALU.mult, ALU.add).then_inc(s_f, 1)
                counts[s_f] += 1
            o_lo(7)
            for j in range(4):
                dve.wait_ge(s_lf, 4 + j + 1)
                link(dve.tensor_tensor_scan(bb[:, j, :], cmask[:], bb[:, j, :], 0.0, ALU.mult, ALU.add), s_b)

            def exponents(i):
                j, m = i // 8, 1 << (i % 8 - 1)
                b, e = halves(bb[:, j, :], m), halves(ee[:, i % 3, :], m)
                middle = b[:, :, 0, m - 1:m].to_broadcast([P, SEQ // (2 * m), m])
                if i >= 3:
                    dve.wait_ge(s_lv, i - 2)
                dve.tensor_tensor(e[:, :, 0, :], middle, b[:, :, 0, :], ALU.subtract)
                dve.tensor_tensor(e[:, :, 1, :], b[:, :, 1, :], middle, ALU.subtract).then_inc(s_dif, 1)

            def times_keys(i):
                j, m = i // 8, 1 << (i % 8 - 1)
                dve.wait_ge(s_e, 7 * j + i % 8)
                low = halves(ee[:, i % 3, :], m)[:, :, 0, :]
                dve.tensor_tensor(low, low, halves(kk[:, j, :], m)[:, :, 0, :], ALU.mult).then_inc(s_ek, 1)

            def collect(i):
                j, lv = i // 8, i % 8
                dve.wait_ge(s_lv, i + 1)
                if lv == 0 and j >= 2:
                    dve.wait_ge(s_pvh, j - 1)
                if lv:
                    dve.wait_ge(s_cp, i)
                d = acc[:, j % 2]
                src = chunks(ps[:, 4 + i % 2, :])
                if lv == 0:
                    dve.tensor_tensor(d, src, ident[:, None, :].to_broadcast([P, TT, P]), ALU.mult).then_inc(s_cp, 1)
                else:
                    dve.copy_predicated(d, lmask[:, lv - 1:lv, :].to_broadcast([P, TT, P]), src).then_inc(s_cp, 1)

            def between(j):
                b, k, q = chunks(bb[:, j, :]), chunks(kk[:, j, :]), chunks(qq[:, j, :])
                if j:
                    dve.wait_ge(s_ofp, j)
                dve.tensor_tensor(kd[:], b[:, 0:3, P - 1:P].to_broadcast([P, 3, P]), b[:, 0:3, :],
                                  ALU.subtract).then_inc(s_of, 1)
                dve.wait_ge(s_ofe, 2 * j + 2)
                dve.tensor_tensor(kd[:], kd[:], k[:, 0:3, :], ALU.mult)
                for at, c in ((0, 0), (3, 1), (5, 2)):
                    dve.tensor_tensor(qs[:, at, :], q[:, c + 1, :], eb[:, c, :], ALU.mult).then_inc(s_ofk, 1)
                dve.wait_ge(s_ofk, 6 * j + 3)
                dve.tensor_scalar(qs[:, 4, :], qs[:, 5, :], eb[:, 1, P - 1:P], None, ALU.mult).then_inc(s_ofk, 1)
                dve.tensor_scalar(qs[:, 1, :], qs[:, 3, :], eb[:, 0, P - 1:P], None, ALU.mult).then_inc(s_ofk, 1)
                dve.wait_ge(s_ofk, 6 * j + 5)
                dve.tensor_scalar(qs[:, 2, :], qs[:, 4, :], eb[:, 0, P - 1:P], None, ALU.mult).then_inc(s_ofk, 1)

            def after(i):
                j, lv = i // 8, i % 8
                if lv == 4:
                    dve.wait_ge(s_stat, STATS[2] + 8 + j + 1)
                    variance(ps[:, 7, 0:TT], P, 0)
                if lv == 5:
                    spread(5 + j)
                if lv == 7:
                    dve.wait_ge(s_rb, 5 + j)
                    dve.scalar_tensor_tensor(kk[:, j, :], htmp[:, j % 2, :], par[:, 0, C_HG:C_HG + 1],
                                             ps[:, 7, :], ALU.mult, ALU.mult).then_inc(s_yn, 1)

            dve.wait_ge(s_po, 8)
            for i in range(34):
                if i < 32 and i % 8:
                    exponents(i)
                if 1 <= i < 33 and (i - 1) % 8:
                    times_keys(i - 1)
                if i >= 2:
                    collect(i - 2)
                if i < 32 and i % 8 == 0:
                    between(i // 8)
                if 8 <= i < 32:
                    after(i - 8)
            for i in (28, 29, 31):
                after(i)
            for j in range(4):
                dve.wait_ge(s_gsil, j + 1)
                dve.wait_ge(s_yn, j + 1)
                dve.tensor_tensor(kk[:, j, :], kk[:, j, :], aq[:, j, :], ALU.mult).then_inc(s_g2, 1)
            for j in range(4):
                dve.wait_ge(s_g2hi, j + 1)
                dve.tensor_tensor(h_lo[:, j, :], kk[:, j, :], h_hi[:, j, :].bitcast(F32),
                                  ALU.subtract).then_inc(s_g2lo, 1)

            for m in range(KD):
                residual(m, m % 4, s_used, U_OUT2 + m + 1)
            norm(3, STATS[3] + 8, 9, C_NF)
            ffn(1)
            down(1, U_END)
            norm(4, STATS[4] + 8, 10, None)
            dve.wait_ge(s_rstd, 10)
            for done, n in enumerate(OUT_ORDER):
                dve.wait_ge(s_ft, done + 1)
                dve.tensor_scalar(obuf[:, n, :], ps[:, n, :], rstd[:, n // 2:n // 2 + 1], None,
                                  ALU.mult).then_inc(s_fin, 1)

        @block.tensor
        def _(pe):
            def unit_mms(bank, at, k, first, last, hi=h_hi, lo=h_lo, used=False):
                whi, wlo = (unit_view(w, at, False)[:, k, :] for w in (w_hi, w_lo))
                pe.matmul(ps[:, bank, :], whi, hi[:, k, :], start=first, stop=False, skip_group_check=True)
                pe.matmul(ps[:, bank, :], whi, lo[:, k, :], start=False, stop=False, skip_group_check=True)
                mm = pe.matmul(ps[:, bank, :], wlo, hi[:, k, :], start=False, stop=last, skip_group_check=True)
                if used:
                    mm.then_inc(s_used, 1)

            def unit(at, bank, i=0, order=range(KD)):
                pe.wait_ge(s_lo, at + 4 * i + 1)
                for n, k in enumerate(order):
                    unit_mms(bank, at, k, n == 0, n == KD - 1, used=(n == KD - 1))

            def pair_first(at, n, banks):
                pe.wait_ge(s_lo, at + 2)
                for k in range(KD):
                    pe.wait_ge(s_hlo, KD * n + k + 1)
                    for c in range(2):
                        unit_mms(banks[c], at + c, k, k == 0, k == KD - 1, used=(k == KD - 1))

            def first_quad(at, n, free):
                for c in range(2):
                    free(c)
                pair_first(at, n, (0, 1))
                for c in (2, 3):
                    free(c)
                    unit(at + c, c)

            pe.wait_ge(s_const, 4)
            for m in range(KD):
                if m >= 4:
                    pe.wait_ge(s_xT, m - 3)
                for t in range(TT):
                    if m == 0 and t % 2 == 0:
                        pe.wait_ge(s_xin[t // 2], 16)
                    mm = pe.transpose(ps[:, 4 + m % 4, t * P:(t + 1) * P], xtok[:, t, m * P:(m + 1) * P], ident[:])
                mm.then_inc(s_xp, 1)
            pe.wait_ge(s_prow, 16 * NPROW)
            for t, n in enumerate(PROWS):
                pe.transpose(ps[:, t, 0:n], prow[0:n, t, :], ident[0:n, 0:n]).then_inc(s_pp, 1)

            def spread(n, bank):
                pe.wait_ge(s_diag, n)
                pe.matmul(ps[:, bank, :], ones[:], diag[:].rearrange("p t n -> p (t n)"),
                          start=True, stop=True, skip_group_check=True).then_inc(s_rb, 1)

            pe.wait_ge(s_xT, KD)
            spread(1, 5)
            pe.wait_ge(s_par, 4)
            first_quad(U_IN, 0, lambda c: None)
            with pe.Fori(1, 4) as i:
                for c in range(4):
                    pe.wait_ge(s_take, 4 * i + c - 3)
                    unit(U_IN + c, c, i)

            def values(t, done):
                for k in range(KD):
                    for n, (a, w) in enumerate(((h_hi, w_hi), (h_lo, w_hi), (h_hi, w_lo))):
                        rhs = w[:, :, k * P:(k + 1) * P]
                        mm = pe.matmul(ps[:, t, :].rearrange("p (s n) -> p s n", n=P), a[:, k, t * P:(t + 1) * P], rhs,
                                       start=(k == 0 and n == 0), stop=(k == KD - 1 and n == 2), skip_group_check=True)
                mm.then_inc(done, 1) if t < TT - 1 else mm.then_inc(s_used, 4)

            pe.wait_ge(s_lo, 20)
            for t in range(2):
                pe.wait_ge(s_take, 12 + t + 1)
                values(t, s_vt)
            pe.wait_ge(s_ht, KD)
            for j in range(8):
                pe.wait_ge(s_qsq, j + 1)
                mm = pe.matmul(ps[0:16, 4, :], sel[:, j, :], sqk[:, j, :], start=(j == 0), stop=(j == 7))
            mm.then_inc(s_qst, 1)
            for t in range(2, 4):
                pe.wait_ge(s_take, 12 + t + 1)
                values(t, s_vt)
            pe.wait_ge(s_qv, 5)
            for j in range(8):
                if j >= 4:
                    pe.wait_ge(s_qn, j - 3)
                pe.matmul(ps[:, 4 + j % 4, :], selT[:, j, :], nvar[:, 1, :], start=True, stop=True).then_inc(s_qb, 1)
            pe.wait_ge(s_qn, 8)
            pe.wait_ge(s_vc, 4)

            def scores(h):
                j, lo = h // 2, 64 * (h % 2)
                if h >= 2:
                    pe.wait_ge(s_w, h - 1)
                for b in range(4):
                    mm = pe.matmul(zps(h)[:, ZOFF[b]:ZOFF[b] + ZLEN[b]], qk[lo:lo + 64, 4 + j, b * P:(b + 1) * P],
                                   qk[lo:lo + 64, j, b * P:SEQ], start=(b != 3), stop=False, skip_group_check=True)
                mm.then_inc(s_z, 1)

            def tails(h):
                pe.wait_ge(s_spl, h + 1)
                for b in range(4):
                    for b2 in range(b, 4):
                        o = ZOFF[b] + P * (b2 - b)
                        for part in (sp_hi, sp_lo):
                            mm = pe.matmul(zps(h)[:, o:o + ZLEN[b2]], (ntri if b2 == b else nones)[:],
                                           part[:, h % 2, ZOFF[b2]:ZOFF[b2] + ZLEN[b2]],
                                           start=False, stop=False, skip_group_check=True)
                mm.then_inc(s_tail, 1)

            def outputs(h):
                j, lo = h // 2, 64 * (h % 2)
                pe.wait_ge(s_w, h + 1)
                if h >= 2 and h % 2 == 0:
                    pe.wait_ge(s_mlo, j)
                for b in range(4):
                    mm = pe.matmul(ps[lo:lo + 64, 6, b * P:SEQ], vtok[:, b, h * 64:(h + 1) * 64],
                                   zl[:, h % 3, ZOFF[b]:ZOFF[b] + ZLEN[b]], start=(b == 0), stop=(b == 3),
                                   skip_group_check=True)
                mm.then_inc(s_pv, 1)

            def sums(bank, src, start, done):
                for t in range(TT):
                    mm = pe.matmul(ps[:, bank, t:t + 1], src[:, t * P:(t + 1) * P], ones[:, 0:1],
                                   start=(start and t == 0), stop=done, skip_group_check=True)
                mm.then_inc(s_stat, 1)

            ln_sq = [sq[:, 0, :], sq[:, 1, :], htmp[:, 0, :], htmp[:, 1, :]]
            pe.wait_ge(s_cdve, 2)
            for s in range(AH + 2):
                if s < AH:
                    scores(s)
                if s == 1:
                    pe.wait_ge(s_tap, 4 * CK)
                    for c in range(CT):
                        mm = pe.matmul(ps[:, 7, :], lnone[:], cy[:, c, :], start=(c == 0), stop=(c == 3))
                    mm.then_inc(s_mean, 1)
                if s == 3:
                    pe.wait_ge(s_cen, CT)
                    for c in range(CT):
                        pe.wait_ge(s_csq, c + 1)
                        sums(7, ln_sq[c], c == 0, c == CT - 1)
                if s == 5:
                    spread(2, 7)
                if 1 <= s <= AH:
                    tails(s - 1)
                if s >= 2:
                    outputs(s - 2)

            def stream_sums(n, m):
                pe.wait_ge(s_sq, 8 * (n - 1) + m + 1)
                sums(4, sq[:, m % 2, :], m == 0, m == KD - 1)

            pe.wait_ge(s_w, AH)
            pe.wait_ge(s_mlo, 8)
            for m in range(KD):
                if m >= 4:
                    pe.wait_ge(s_x, m - 3)
                unit(U_OUT + m, m % 4)
                if m >= 1:
                    stream_sums(1, m - 1)
            stream_sums(1, KD - 1)
            spread(3, 5)

            def ffn(lay, u0, n):
                first_quad(u0, n, lambda c: pe.wait_ge(s_x, 16 * lay + 8))
                with pe.Fori(1, NUP) as i:
                    for c in range(4):
                        pe.wait_ge(s_conv if c < 2 else s_gv, KF * lay + 2 * i + c % 2 - 1)
                        unit(u0 + c, c, i)

            def down(lay, u0, n, m_done):
                def ktile(at, k, i=0, first=False, last=False):
                    pe.wait_ge(s_lo, at + 4 * i + 1)
                    pe.wait_ge(s_alo, KF * lay + k + 1)
                    hi, lo = (a[:, bass.ds(k, 1), :].rearrange("p a n -> p (a n)") for a in (a_hi, a_lo))
                    whi, wlo = (unit_view(w, at, True) for w in (w_hi, w_lo))
                    for m in range(KD):
                        b = (m + 4) % 8
                        if first and m == 4:
                            pe.wait_ge(s_conv, KF * (lay + 1))
                        if first and m == 6:
                            pe.wait_ge(s_gv, KF * (lay + 1))
                        for w, a, st in ((whi, hi, first), (whi, lo, False), (wlo, hi, False)):
                            mm = pe.matmul(ps[:, b, :], w[:, m * P:(m + 1) * P], a, start=st, stop=False,
                                           skip_group_check=True)
                        if m == KD - 1:
                            mm.then_inc(s_used, 1)
                        elif last:
                            mm.then_inc(s_out, 1)
                        if last and m >= 2:
                            if m == 2:
                                pe.wait_ge(s_x, 16 * lay + 8 + 1)
                            stream_sums(m_done, m - 2)
                pe.wait_ge(s_ht, KD * (n + 1))
                for c in range(4):
                    ktile(u0 + c, c, first=(c == 0))
                with pe.Fori(1, 5) as i:
                    for c in range(4):
                        ktile(u0 + c, 4 * i + c, i)
                for k in range(20, KF):
                    ktile(u0 + k, k, last=(k == KF - 1))
                stream_sums(m_done, KD - 2)
                stream_sums(m_done, KD - 1)

            ffn(0, U_UP, 1)
            down(0, U_DOWN, 1, 2)

            spread(4, 5)
            pe.wait_ge(s_x, 16)
            pair_first(U_IN2, 2, (2, 3))
            for c in range(4):
                if c >= 2:
                    pe.wait_ge(s_take2, c - 1)
                unit(U_IN2 + 2 + c, c)
                if c == 0:
                    pe.wait_ge(s_take2, 2)
                    for t in range(TT):
                        mm = pe.transpose(ps[:, 6, t * P:(t + 1) * P], vT[:, t * P:(t + 1) * P], ident[:])
                    mm.then_inc(s_vtp, 1)

            def sliding_scores(n):
                b, g = n // 2, n % 2
                if n:
                    pe.wait_ge(s_sm, n)
                for a in range(4):
                    half, tile = a % 2, 2 * g + a // 2
                    k0 = max(b - 1, 0) * P
                    kn = (b + 1) * P - k0
                    o = ps[:, 4 + half, (a // 2) * 2 * P:(a // 2 + 1) * 2 * P][:, 2 * P - kn:]
                    mm = pe.matmul(o, aq[64 * half:64 * half + 64, tile, b * P:(b + 1) * P],
                                   kT[64 * half:64 * half + 64, (half + g) % 2, k0:k0 + kn],
                                   start=(a < 2), stop=True, skip_group_check=True)
                mm.then_inc(s_sc, 1)

            def sliding_transposes(n):
                pe.wait_ge(s_p, n + 1)
                if n:
                    pe.wait_ge(s_olo, n)
                for half in range(1 if n < 2 else 0, 2):
                    for a in range(4):
                        mm = pe.transpose(ps[:, 6 + half, a * P:(a + 1) * P], sm[:, n % 2, a, half * P:(half + 1) * P], ident[:])
                mm.then_inc(s_tr, 1)

            def sliding_outputs(n):
                b, g = n // 2, n % 2
                pe.wait_ge(s_pT, n + 1 if n < 2 else 2 * n)
                first = 1 if n < 2 else 0
                for par2 in range(2):
                    for half in range(first, 2):
                        mm = pe.matmul(ps[64 * par2:64 * par2 + 64, 6, 0:2 * P],
                                       vt2[:, b - 1 + half, 64 * g:64 * g + 64],
                                       pT[:, n % 2, half, 2 * P * par2:2 * P * (par2 + 1)],
                                       start=(half == first), stop=(half == 1), skip_group_check=True)
                mm.then_inc(s_po, 1)

            pe.wait_ge(s_take2, 6)
            pe.wait_ge(s_ks, 32)
            pe.wait_ge(s_vt2, 1)
            for n in range(8):
                sliding_scores(n)
                if n:
                    sliding_outputs(n - 1)
                pe.wait_ge(s_take2, n + 3)
                unit(U_IN2 + 6 + n, n % 4)
                sliding_transposes(n)
            sliding_outputs(7)

            def level(i):
                j, lv = i // 8, i % 8
                if i >= 2:
                    pe.wait_ge(s_cp, i - 1)
                if lv:
                    pe.wait_ge(s_ek, 7 * j + lv)
                    pe.wait_ge(s_eq, 7 * j + lv)
                    k = q = ee[:, i % 3, :]
                else:
                    pe.wait_ge(s_f, 2 * j + 2)
                    k, q = kk[:, j, :], qq[:, j, :]
                for c in range(TT):
                    mm = pe.matmul(ps[:, 4 + i % 2, c * P:(c + 1) * P], k[:, c * P:(c + 1) * P], q[:, c * P:(c + 1) * P],
                                   start=(c == 0), stop=True, skip_group_check=True)
                mm.then_inc(s_lv, 1)

            def between(j):
                pe.wait_ge(s_ofk, 6 * j + 6)
                if j:
                    pe.wait_ge(s_yn, j)
                else:
                    pe.wait_ge(s_olo, 8)
                for bank, c0, s_, at, n in ((6, 0, 0, 0, 3), (6, 3, 2, 5, 1), (7, 0, 1, 3, 2)):
                    mm = pe.matmul(ps[:, bank, c0 * P:(c0 + n) * P], kd[:, s_, :],
                                   qs[:, at:at + n, :].rearrange("p c n -> p (c n)"),
                                   start=(c0 == 0), stop=True, skip_group_check=True)
                mm.then_inc(s_ofp, 1)

            OFF_AT = (0, 4, 3)

            def after(i):
                j, lv = i // 8, i % 8
                if lv == 1:
                    pe.wait_ge(s_ofc, 2 * j + 2)
                    pe.wait_ge(s_cp, 8 * j + 8)
                    pe.wait_ge(s_take2, 18)
                    for s_ in range(TT):
                        w = vh[:, s_, j * P:(j + 1) * P]
                        mm = pe.matmul(ps[:, 6, s_ * P:(s_ + 1) * P], w, acc[:, j % 2, s_, :],
                                       start=(s_ == 0), stop=False, skip_group_check=True)
                        n = TT - 1 - s_
                        if n:
                            pe.matmul(ps[:, 6, (s_ + 1) * P:], w,
                                      off[:, j % 2, OFF_AT[s_]:OFF_AT[s_] + n, :].rearrange("p c n -> p (c n)"),
                                      start=False, stop=False, skip_group_check=True)
                    mm.then_inc(s_pvh, 1)
                if lv == 3:
                    pe.wait_ge(s_oc, 2 * j + 2)
                    sums(7, sq[:, j % 2, :], True, True)
                if lv == 6:
                    spread(5 + j, 7)

            for i in range(32):
                if i + 1 in FILL:
                    t = FILL.index(i + 1)
                    if t < 4:
                        if t == 0:
                            pe.wait_ge(s_lo, U_IN2 + 18)
                        pe.wait_ge(s_take2, 10 + t + 1)
                        values(t, s_vh)
                    else:
                        pe.wait_ge(s_take2, 14 + t - 3)
                        unit(U_IN2 + 14 + t, t - 4)
                level(i)
                if i >= 8:
                    after(i - 8)
                if i % 8 == 7:
                    between(i // 8)
            for i in (25, 27, 30):
                after(i)

            def unit2(m, ks, first, last):
                for k in ks:
                    t_hi, t_lo, at = (h_hi, h_lo, k) if k < 4 else (m_hi, m_lo, k - 4)
                    whi, wlo = (unit_view(w, U_OUT2 + m, False)[:, k, :] for w in (w_hi, w_lo))
                    for n, (w, a) in enumerate(((whi, t_hi), (whi, t_lo), (wlo, t_hi))):
                        mm = pe.matmul(ps[:, m % 4, :], w, a[:, at, :], start=(first and k == ks[0] and n == 0),
                                       stop=(last and k == ks[-1] and n == 2), skip_group_check=True)
                if last:
                    mm.then_inc(s_used, 1)

            pe.wait_ge(s_take2, 22)
            pe.wait_ge(s_olo, 8)
            for m in range(4):
                pe.wait_ge(s_lo, U_OUT2 + m + 1)
                unit2(m, (4, 5, 6, 7), True, False)
            pe.wait_ge(s_g2lo, 4)
            for m in range(KD):
                if m < 4:
                    unit2(m, (0, 1, 2, 3), False, True)
                else:
                    pe.wait_ge(s_x, 16 + m - 3)
                    pe.wait_ge(s_lo, U_OUT2 + m + 1)
                    unit2(m, (4, 5, 6, 7, 0, 1, 2, 3), True, True)
                if m >= 1:
                    stream_sums(3, m - 1)
            stream_sums(3, KD - 1)
            spread(9, 5)
            ffn(1, U_UP2, 3)
            down(1, U_DOWN2, 3, 4)

            pe.wait_ge(s_x, 32)
            for n in OUT_ORDER:
                if n == 4:
                    pe.wait_ge(s_var, 10)
                t, half = n // 2, n % 2
                for f in range(4):
                    m = 4 * half + f
                    pe.wait_ge(s_gx, m + 1)
                    mm = pe.transpose(ps[:, n, f * P:(f + 1) * P], xT[:, m, t * P:(t + 1) * P], ident[:])
                mm.then_inc(s_ft, 1)


_INS = ["x", "norm1_g", "w_in", "q_norm_g", "k_norm_g", "conv_dw_w", "conv_dw_b", "conv_ln_g", "conv_ln_b", "w_out",
        "norm2_g", "w_up", "ffn_dw_w", "ffn_dw_b", "w_down", "norm_mix_w_2", "w_in_2", "b_attn_2", "lb_logits_2",
        "hg_norm_w_2", "sinks_2", "w_out_2", "norm_ffn_w_2", "w_gate_2", "w_up_2", "conv_w_2", "conv_b_2",
        "w_down_2", "final_norm_w_2"]


def kernel(**inputs):
    import numpy as np
    import concourse.bacc as bacc
    from concourse.bass_utils import run_bass_kernel_spmd

    nc = bacc.Bacc("TRN2", target_bir_lowering=False, num_devices=1)
    arrays, args = {}, []
    for name in _INS:
        a = np.ascontiguousarray(inputs[name])
        arrays[f"in_{name}"] = a
        args.append(nc.dram_tensor(f"in_{name}", a.shape, mybir.dt.from_np(a.dtype), kind="ExternalInput").ap())
    args.append(nc.dram_tensor("out_dram", (1, SEQ, DM), F32, kind="ExternalOutput").ap())
    hybrid_blocks_kernel(nc, *args)
    r = run_bass_kernel_spmd(nc, [arrays], core_ids=[0])
    return r.results[0]["out_dram"]
```

```python
from contextlib import ExitStack

import concourse.bass as bass
from concourse import mybir

ALU = mybir.AluOpType
ACT = mybir.ActivationFunctionType
F32 = mybir.dt.float32
F32R = mybir.dt.float32r
I32 = mybir.dt.int32
AX = mybir.AxisListType

P = 128
SEQ = 512
TT = SEQ // P
DM = 1024
KD = DM // P
DFF = 2816
KF = DFF // P
NUP = KF // 2
EPS = 1e-6
CK = 31
CT = 4
PAD = CK - 1
NEG = -1e30

U_IN, U_OUT, U_UP, U_DOWN = 0, 20, 28, 72
U_IN2, U_OUT2, U_UP2, U_DOWN2, U_END = 94, 116, 124, 168, 190

C_N1, C_N2, C_NM, C_NF = 0, 8, 16, 24
C_CB, C_LG, C_LB, C_LL, C_HG = 32, 36, 40, 44, 52
C_FB, C_FB2, C_QG, C_KG, C_BA, C_FN = 53, 75, 97, 98, 99, 105
PROWS = (113, 66, 66, 124)
NPROW = 20

OUT_BANK = (0, 1, 2, 7, 0, 1, 2, 3)
AH = 8
LN_STEPS = 14
GC = 27
FILL = (1, 3, 5, 7, 12, 17, 22, 27)
FILL_K = (4, 4) * 4 + (2, 2, 1, 2, 1) * 4
STATS = (0, 1, 4, 11, 14)

OUT_TILES = ((0, 0, 5), (1, 0, 6), (2, 0, 7), (3, 0, 0), (0, 1, 1), (1, 1, 2), (2, 1, 3), (3, 1, 4))

ZOFF = (0, 640, 1024, 512)
ZLEN = (512, 384, 256, 128)
ZW = 1280


def hybrid_blocks_kernel(
    nc, x, norm1_g, w_in, q_norm_g, k_norm_g, conv_dw_w, conv_dw_b, conv_ln_g, conv_ln_b, w_out,
    norm2_g, w_up, ffn_dw_w, ffn_dw_b, w_down, norm_mix_w_2, w_in_2, b_attn_2, lb_logits_2,
    hg_norm_w_2, sinks_2, w_out_2, norm_ffn_w_2, w_gate_2, w_up_2, conv_w_2, conv_b_2, w_down_2,
    final_norm_w_2, out,
):
    with ExitStack() as ctx:
        def sb(name, shape, dt=F32, stack=ctx):
            return stack.enter_context(nc.sbuf_tensor(name, shape, dt))

        def sem(name):
            return ctx.enter_context(nc.semaphore(name))

        xT = sb("xT", [P, KD, SEQ])
        h_hi = sb("h_hi", [P, KD, SEQ], F32R)
        h_lo = sb("h_lo", [P, KD, SEQ], F32R)
        w_raw = sb("w_raw", [P, 2, 2 * DM])
        w_hi = sb("w_hi", [P, 4, DM], F32R)
        w_lo = sb("w_lo", [P, 4, DM], F32R)
        ident = sb("ident", [P, P])
        ones = sb("ones", [P, P])
        par = sb("par", [P, 4, P])
        stat = sb("stat", [P, 4])
        rstd = sb("rstd", [P, 4])
        ss0 = sb("ss0", [P, 4])
        sinkb = sb("sinkb", [P, 8])
        mhalf = sb("mhalf", [P, 4])
        sq = sb("sq", [P, 2, SEQ])
        diag = sb("diag", [P, TT, P])
        htmp = sb("htmp", [P, 2, SEQ])

        with ExitStack() as early:
            glu = sb("glu", [P, CT, PAD + SEQ + 2], stack=early)
            cy = sb("cy", [P, CT, SEQ], stack=early)
            qk = sb("qk", [P, 8, SEQ], stack=early)
            vtok = sb("vtok", [P, TT, SEQ], stack=early)
            sel = sb("sel", [P, 8, 16], stack=early)
            selT = sb("selT", [16, 8, P], stack=early)
            nvar = sb("nvar", [16, 3, SEQ], stack=early)
            gq8 = sb("gq8", [P, 1], stack=early)
            lnone = sb("lnone", [P, P], stack=early)
            smask = sb("smask", [P, P], stack=early)
            nmask = sb("nmask", [P, P], stack=early)
            ntri_f = sb("ntri_f", [P, P], stack=early)
            ntri = sb("ntri", [P, P], F32R, stack=early)
            nones = sb("nones", [P, P], F32R, stack=early)
            with ExitStack() as start:
                xtok = sb("xtok", [P, TT, DM], stack=start)
                xjunk = sb("xjunk", [P, DM], stack=start)
                prow = sb("prow", [P, 4, P], stack=start)
            with ExitStack() as projecting:
                sqk = sb("sqk", [P, 8, SEQ], stack=projecting)
            zl = sb("zl", [P, 3, ZW], stack=early)
            sp_hi = sb("sp_hi", [P, 2, ZW], F32R, stack=early)
            sp_lo = sb("sp_lo", [P, 2, ZW], F32R, stack=early)
        with ExitStack() as mid:
            m_hi = sb("m_hi", [P, 4, SEQ], F32R, stack=mid)
            m_lo = sb("m_lo", [P, 4, SEQ], F32R, stack=mid)
            kT = sb("kT", [P, 2, SEQ], stack=mid)
            vT = sb("vT", [P, SEQ], stack=mid)
            vt2 = sb("vt2", [P, TT, P], stack=mid)
            aq = sb("aq", [P, 4, SEQ], stack=mid)
            kk = sb("kk", [P, 4, SEQ], stack=mid)
            qq = sb("qq", [P, 4, SEQ], stack=mid)
            bb = sb("bb", [P, 4, SEQ], stack=mid)
            vh = sb("vh", [P, TT, SEQ], stack=mid)
            lmask = sb("lmask", [P, 7, P], I32, stack=mid)
            cmask = sb("cmask", [P, SEQ], stack=mid)
            band = sb("band", [P, 2 * P], stack=mid)
            lbt = sb("lbt", [P, 6, 4], stack=mid)
            with ExitStack() as sliding:
                sm = sb("sm", [P, 2, 4, 2 * P], stack=sliding)
                pT = sb("pT", [P, 2, 2, SEQ], stack=sliding)
                smx = sb("smx", [P, 2, 6, 4], stack=sliding)
            ee = sb("ee", [P, 3, SEQ], stack=mid)
            acc = sb("acc", [P, 2, TT, P], stack=mid)
            eb = sb("eb", [P, 3, P], stack=mid)
            kd = sb("kd", [P, 2, 3, P], stack=mid)
            qs = sb("qs", [P, 6, P], stack=mid)
            off = sb("off", [P, 2, 6, P], stack=mid)
        with ExitStack() as late:
            obuf = sb("obuf", [P, 8, SEQ], stack=late)
        a_hi = sb("a_hi", [P, KF, SEQ], F32R)
        a_lo = sb("a_lo", [P, KF, SEQ], F32R)
        cv = sb("cv", [P, 2, SEQ])

        ps = ctx.enter_context(nc.psum_tensor("ps", [P, 8, SEQ], F32))

        s_raw = [sem(f"s_raw{n}") for n in range(2)]
        s_hi = sem("s_hi")
        s_lo = sem("s_lo")
        s_used = sem("s_used")
        s_const = sem("s_const")
        s_cdve = sem("s_cdve")
        s_prow = sem("s_prow")
        s_xin = [sem(f"s_xin{n}") for n in range(2)]
        s_pp = sem("s_pp")
        s_par = sem("s_par")
        s_xp = sem("s_xp")
        s_xT = sem("s_xT")
        s_ss0 = sem("s_ss0")
        s_x = sem("s_x")
        s_sq = sem("s_sq")
        s_acc = sem("s_acc")
        s_stat = sem("s_stat")
        s_var = sem("s_var")
        s_rstd = sem("s_rstd")
        s_diag = sem("s_diag")
        s_rb = sem("s_rb")
        s_ht = sem("s_ht")
        s_hhi = sem("s_hhi")
        s_hlo = sem("s_hlo")
        s_take = sem("s_take")
        s_glu = sem("s_glu")
        s_tap = sem("s_tap")
        s_qsq = sem("s_qsq")
        s_qst = sem("s_qst")
        s_qv = sem("s_qv")
        s_qr = sem("s_qr")
        s_qb = sem("s_qb")
        s_qn = sem("s_qn")
        s_vt = sem("s_vt")
        s_vc = sem("s_vc")
        s_z = sem("s_z")
        s_ab = sem("s_ab")
        s_l = sem("s_l")
        s_sp = sem("s_sp")
        s_spl = sem("s_spl")
        s_tail = sem("s_tail")
        s_dm = sem("s_dm")
        s_w = sem("s_w")
        s_pv = sem("s_pv")
        s_mhi = sem("s_mhi")
        s_mlo = sem("s_mlo")
        s_ln = sem("s_ln")
        s_mean = sem("s_mean")
        s_lc = sem("s_lc")
        s_ly = sem("s_ly")
        s_ls = sem("s_ls")
        s_clo = sem("s_clo")
        s_out = sem("s_out")
        s_t0 = sem("s_t0")
        s_tp = sem("s_tp")
        s_conv = sem("s_conv")
        s_silu = sem("s_silu")
        s_gv = sem("s_gv")
        s_ahi = sem("s_ahi")
        s_alo = sem("s_alo")
        s_sink = sem("s_sink")
        s_take2 = sem("s_take2")
        s_ks = sem("s_ks")
        s_vtp = sem("s_vtp")
        s_vt2 = sem("s_vt2")
        s_gc = sem("s_gc")
        s_lb = sem("s_lb")
        s_sc = sem("s_sc")
        s_sm = sem("s_sm")
        s_mx = sem("s_mx")
        s_pe = sem("s_pe")
        s_den = sem("s_den")
        s_p = sem("s_p")
        s_tr = sem("s_tr")
        s_pT = sem("s_pT")
        s_po = sem("s_po")
        s_ohi = sem("s_ohi")
        s_olo = sem("s_olo")
        s_f = sem("s_f")
        s_lf = sem("s_lf")
        s_b = sem("s_b")
        s_dif = sem("s_dif")
        s_e = sem("s_e")
        s_ek = sem("s_ek")
        s_eq = sem("s_eq")
        s_lv = sem("s_lv")
        s_cp = sem("s_cp")
        s_of = sem("s_of")
        s_ofe = sem("s_ofe")
        s_ofk = sem("s_ofk")
        s_ofp = sem("s_ofp")
        s_ofc = sem("s_ofc")
        s_pvh = sem("s_pvh")
        s_oc = sem("s_oc")
        s_yn = sem("s_yn")
        s_g2 = sem("s_g2")
        s_g2hi = sem("s_g2hi")
        s_g2lo = sem("s_g2lo")
        s_vh = sem("s_vh")
        s_gsil = sem("s_gsil")
        s_gx = sem("s_gx")
        s_ft = sem("s_ft")
        s_fin = sem("s_fin")
        s_fin2 = sem("s_fin2")
        s_st = sem("s_st")

        def halves(t, m):
            return t.rearrange("p (n two m) -> p n two m", two=2, m=m)

        def chunks(t):
            return t.rearrange("p (c n) -> p c n", n=P)

        def zps(h):
            b = 3 * (h % 2)
            return ps[:, b:b + 3, :].rearrange("p b n -> p (b n)")[:, 0:ZW]

        def unit_raw(u, down):
            pair = w_raw[:, (u // 2) % 2, :]
            if down:
                return pair.rearrange("p (c n) -> p c n", c=2)[:, u % 2, :]
            return pair.rearrange("p (k c n) -> p k c n", k=KD, c=2)[:, :, u % 2, :]

        def unit_view(t, u, down):
            w = t[:, u % 4, :]
            return w if down else w.rearrange("p (k n) -> p k n", k=KD)

        def is_down(u):
            return U_DOWN <= u < U_IN2 or U_DOWN2 <= u < U_END

        block = ctx.enter_context(nc.Block())

        @block.sync
        def _(sp):
            def pair(p, src, at=None, first=False):
                slot = p % 2 if at is None else at
                if not first:
                    sp.wait_ge(s_lo, 2 * p - 2)
                sp.dma_start(w_raw[:, slot, :].rearrange("p (k n) -> p k n", n=src.shape[-1]),
                             src).then_inc(s_raw[slot], 16)

            def cols(w, c0):
                return w[0].rearrange("(k p) n -> p k n", p=P)[:, :, bass.ds(c0, 2 * P)]

            def rows(w, k0):
                return w[0].rearrange("(k p) n -> p k n", p=P)[:, bass.ds(k0, 2), :]

            for n in range(2):
                sp.dma_start(xtok[:, 2 * n:2 * n + 2, :],
                             x[0, 2 * n * P:2 * (n + 1) * P, :].rearrange("(t p) d -> p t d", p=P)).then_inc(s_xin[n], 16)
            A0, B0, V0 = 1536, 2048, 1024
            in_cols = [B0, A0, B0 + 256, A0 + 256, 0, 256, 512, 768, V0, V0 + 256]
            pair(0, cols(w_in, in_cols[0]), first=True)

            def row(t, r0, src, c0=0):
                sp.dma_start(prow[r0:r0 + src.shape[0], t, c0:c0 + src.shape[1]], src).then_inc(s_prow, 16)
            for r0, a in ((C_N1, norm1_g), (C_N2, norm2_g), (C_NM, norm_mix_w_2), (C_NF, norm_ffn_w_2),
                          (C_CB, conv_dw_b), (C_LG, conv_ln_g), (C_LB, conv_ln_b), (C_LL, lb_logits_2),
                          (C_HG, hg_norm_w_2), (C_FB, ffn_dw_b), (C_FB2, conv_b_2), (C_BA, b_attn_2),
                          (C_FN, final_norm_w_2.rearrange("(l n) -> l n", l=1))):
                row(0, r0, a.rearrange("l (c p) -> (l c) p", p=P))
            for r0, a in ((C_QG, q_norm_g), (C_KG, k_norm_g)):
                row(0, r0, a, 0)
                row(0, r0, a, 64)
            for t, a in ((1, ffn_dw_w), (2, conv_w_2), (3, conv_dw_w)):
                row(t, 0, a.rearrange("l k (c p) -> (l k c) p", p=P))

            sp.dma_start(sinkb[:], sinks_2.to_broadcast([P, 8])).then_inc(s_sink, 16)
            for n, c0 in enumerate(in_cols[1:]):
                pair(n + 1, cols(w_in, c0), first=n == 0)
            for n in range(4):
                pair(U_OUT // 2 + n, cols(w_out, 256 * n))

            def up(gate, val, v0, u0):
                with sp.Fori(0, NUP) as i:
                    pair(u0 // 2 + 2 * i, cols(gate, 256 * i), at=(u0 // 2) % 2)
                    pair(u0 // 2 + 1 + 2 * i, cols(val, v0 + 256 * i), at=(u0 // 2 + 1) % 2)

            def down(w, u0):
                pair(u0 // 2, rows(w, 0))
                with sp.Fori(0, 5) as i:
                    pair(u0 // 2 + 1 + 2 * i, rows(w, 4 * i + 2), at=(u0 // 2 + 1) % 2)
                    pair(u0 // 2 + 2 + 2 * i, rows(w, 4 * i + 4), at=(u0 // 2) % 2)

            up(w_up, w_up, DFF, U_UP)
            down(w_down, U_DOWN)
            for n, c0 in enumerate((2560, 2048, 2304, 512, 768, 0, 256, 1024, 1280, 1536, 1792)):
                pair(U_IN2 // 2 + n, cols(w_in_2, c0))
            for n in range(4):
                pair(U_OUT2 // 2 + n, cols(w_out_2, 256 * n))
            up(w_gate_2, w_up_2, 0, U_UP2)
            down(w_down_2, U_DOWN2)
            for n, (t, half, bank) in enumerate(OUT_TILES):
                sp.wait_ge(s_fin2 if n % 2 else s_fin, n // 2 + 1)
                sp.dma_start(out[0, t * P:(t + 1) * P, 512 * half:512 * (half + 1)],
                             obuf[:, n, :]).then_inc(s_st, 16)
            sp.wait_ge(s_st, 16 * 8)

        @block.gpsimd
        def _(pool):
            pool.memset(ident[:], 0.0).then_inc(s_const, 1)
            pool.memset(ones[:], 1.0).then_inc(s_const, 1)
            pool.memset(mhalf[:], -0.5).then_inc(s_const, 1)
            pool.wait_ge(s_const, 3)
            pool.affine_select(out=ident[:], in_=ident[:], compare_op=ALU.not_equal, fill=1.0, base=0,
                               pattern=[[-1, P]], channel_multiplier=1).then_inc(s_const, 1)
            pool.memset(sel[:], 1.0).then_inc(s_const, 1)
            pool.memset(selT[:], 1.0).then_inc(s_const, 1)
            pool.memset(lnone[:], 1.0 / (CT * P)).then_inc(s_const, 1)
            pool.memset(smask[:], 1.0).then_inc(s_const, 1)
            pool.memset(nmask[:], 0.0).then_inc(s_const, 1)
            pool.memset(ntri_f[:], -1.0).then_inc(s_const, 1)
            pool.memset(glu[:, :, 0:PAD], 0.0).then_inc(s_const, 1)
            pool.wait_ge(s_const, 11)
            pool.affine_select(out=sel[:], in_=sel[:], compare_op=ALU.is_ge, fill=0.0, base=0,
                               pattern=[[P, 8], [-64, 16]], channel_multiplier=1).then_inc(s_const, 1)
            pool.affine_select(out=selT[:], in_=selT[:], compare_op=ALU.is_ge, fill=0.0, base=0,
                               pattern=[[P, 8], [1, P]], channel_multiplier=-64).then_inc(s_const, 1)
            pool.affine_select(out=smask[:], in_=smask[:], compare_op=ALU.is_gt, fill=0.0, base=0,
                               pattern=[[1, P]], channel_multiplier=-1).then_inc(s_const, 1)
            pool.affine_select(out=nmask[:], in_=nmask[:], compare_op=ALU.is_gt, fill=NEG, base=0,
                               pattern=[[1, P]], channel_multiplier=-1).then_inc(s_const, 1)
            pool.affine_select(out=ntri_f[:], in_=ntri_f[:], compare_op=ALU.is_ge, fill=0.0, base=0,
                               pattern=[[-1, P]], channel_multiplier=1).then_inc(s_const, 1)
            pool.wait_ge(s_const, 16)
            pool.affine_select(out=sel[:], in_=sel[:], compare_op=ALU.is_ge, fill=0.0, base=63,
                               pattern=[[-P, 8], [64, 16]], channel_multiplier=-1).then_inc(s_const, 1)
            pool.affine_select(out=selT[:], in_=selT[:], compare_op=ALU.is_ge, fill=0.0, base=63,
                               pattern=[[-P, 8], [-1, P]], channel_multiplier=64).then_inc(s_const, 1)

            def rest(at, i=0):
                pool.wait_ge(s_hi, at + 4 * i + 1)
                down = is_down(at)
                pool.tensor_tensor(unit_view(w_lo, at, down), unit_raw(at, down),
                                   unit_view(w_hi, at, down).bitcast(F32), ALU.subtract).then_inc(s_lo, 1)

            def rests(u0, n):
                if n >= 8:
                    with pool.Fori(0, n // 4) as i:
                        for c in range(4):
                            rest(u0 + c, i)
                    u0, n = u0 + 4 * (n // 4), n % 4
                for c in range(n):
                    rest(u0 + c)

            def inverse_root(n):
                pool.wait_ge(s_var, n)
                pool.tensor_tensor(rstd[:], stat[:], mhalf[:], ALU.pow).then_inc(s_rstd, 1)

            rests(U_IN, 1)
            inverse_root(1)
            rests(U_IN + 1, 3)
            rests(U_IN + 4, 16)
            rests(U_OUT, 4)
            n_ln = [0]
            def step(ins):
                n_ln[0] += 1
                ins.then_inc(s_ln, 1)
                pool.wait_ge(s_ln, n_ln[0])
            total, row = sq[:, 0, :], sq[:, 1, :]
            pool.wait_ge(s_tap, 4 * CK)
            step(pool.tensor_tensor(total, cy[:, 0, :], cy[:, 1, :], ALU.add))
            for c in (2, 3):
                step(pool.tensor_tensor(total, total, cy[:, c, :], ALU.add))
            pool.wait_ge(s_lc, 1)
            for c in range(CT):
                pool.tensor_tensor(cy[:, c, :], cy[:, c, :], row, ALU.subtract).then_inc(s_ln, 1)
                n_ln[0] += 1
            pool.wait_ge(s_ln, n_ln[0])
            step(pool.tensor_tensor(total, cy[:, 0, :], cy[:, 0, :], ALU.mult))
            for c in range(1, CT):
                step(pool.tensor_tensor(htmp[:, c % 2, :], cy[:, c, :], cy[:, c, :], ALU.mult))
                step(pool.tensor_tensor(total, total, htmp[:, c % 2, :], ALU.add))
            assert n_ln[0] == LN_STEPS
            inverse_root(2)
            pool.wait_ge(s_lc, 2)
            for c in range(CT):
                pool.tensor_tensor(cy[:, c, :], cy[:, c, :], row, ALU.mult).then_inc(s_ly, 1)
            for c in range(CT):
                pool.wait_ge(s_mhi, 2 + c + 1)
                pool.tensor_tensor(h_lo[:, CT + c, :], cy[:, c, :], h_hi[:, CT + c, :].bitcast(F32),
                                   ALU.subtract).then_inc(s_clo, 1)
            def add_squares(n, m):
                pool.wait_ge(s_sq, 8 * (n - 1) + m + 1)
                if m > 1:
                    pool.wait_ge(s_acc, 5 * (n - 1) + m - 1)
                pool.tensor_tensor(htmp[:, 0, :], htmp[:, 0, :], sq[:, m % 2, :], ALU.add).then_inc(s_acc, 1)

            def projected(n, u0):
                for m in range(KD - 1):
                    rests(u0 + m, 1)
                    if 1 <= m <= 5:
                        add_squares(n, m)

            projected(1, U_OUT + 4)
            inverse_root(3)
            rests(U_UP + 3, 1)
            rests(U_UP + 4, 40)
            rests(U_DOWN, 22)
            rests(U_IN2, 2)
            for m in range(1, 6):
                add_squares(2, m)
            inverse_root(4)
            rests(U_IN2 + 2, 4)
            pool.wait_ge(s_used, U_IN2)
            steps = [s_gc, 0]
            def link(ins):
                steps[1] += 1
                ins.then_inc(s_gc, 1)
                pool.wait_ge(s_gc, steps[1])
            link(pool.memset(lmask[:], 0))
            for lv in range(7):
                m = 1 << lv
                upper = lmask[:, lv, :].rearrange("p (n two m) -> p n two m", two=2, m=m)[:, :, 1, :]
                n = P // (2 * m)
                link(pool.memset(upper, 1))
                link(pool.affine_select(out=upper, in_=upper, compare_op=ALU.is_ge, fill=0, base=0,
                                        pattern=[[-2 * m, n], [0, m]], channel_multiplier=1))
                link(pool.affine_select(out=upper, in_=upper, compare_op=ALU.is_ge, fill=0, base=m - 1,
                                        pattern=[[2 * m, n], [0, m]], channel_multiplier=-1))
            link(pool.memset(cmask[:], 1.0))
            link(pool.memset(cmask[:, 0:SEQ:P], 0.0))
            link(pool.memset(band[:], 0.0))
            link(pool.affine_select(out=band[:, 0:P], in_=band[:, 0:P], compare_op=ALU.is_gt, fill=NEG, base=0,
                                    pattern=[[1, P]], channel_multiplier=-1))
            link(pool.affine_select(out=band[:, P:], in_=band[:, P:], compare_op=ALU.is_ge, fill=NEG, base=0,
                                    pattern=[[-1, P]], channel_multiplier=1))
            assert steps[1] == GC
            rests(U_IN2 + 6, 12)

            def times_queries(i):
                j, m = i // 8, 1 << (i % 8 - 1)
                pool.wait_ge(s_e, 7 * j + i % 8)
                up = halves(ee[:, i % 3, :], m)[:, :, 1, :]
                pool.tensor_tensor(up, up, halves(qq[:, j, :], m)[:, :, 1, :], ALU.mult).then_inc(s_eq, 1)

            for i in range(32):
                if i > 8 and i % 8 == 5:
                    inverse_root(4 + i // 8)
                if i % 8:
                    times_queries(i)
                if i == 8:
                    rests(U_IN2 + 18, 4)
                if i - 1 in FILL[4:]:
                    rests(U_OUT2 + FILL[4:].index(i - 1), 1)
            inverse_root(8)
            projected(3, U_OUT2 + 4)
            inverse_root(9)
            rests(U_UP2 + 3, 1)
            rests(U_UP2 + 4, 40)
            rests(U_DOWN2, 22)
            for m in range(1, 6):
                add_squares(4, m)
            inverse_root(10)

        @block.scalar
        def _(act):
            def table(n):
                act.add_instruction(mybir.InstLoadActFuncSet(name=nc.get_next_instruction_name(),
                                                             act_func_set_id=n, ins=[], outs=[]))

            def lead(at, i=0):
                act.wait_ge(s_raw[(at // 2) % 2], 16 * (at // 4 + 1) + 16 * i)
                if at >= 4:
                    act.wait_ge(s_used, at + 4 * i - 3)
                down = is_down(at)
                act.activation(unit_view(w_hi, at, down), unit_raw(at, down), ACT.Copy).then_inc(s_hi, 1)

            for t in range(TT):
                act.wait_ge(s_xin[t // 2], 16)
                if t:
                    act.wait_ge(s_ss0, t)
                act.activation(xjunk[:], xtok[:, t, :], ACT.Square, accum_out=ss0[:, t:t + 1]).then_inc(s_ss0, 1)
            for u in range(4):
                lead(u)

            def norm_hi(n):
                for k in range(KD):
                    act.wait_ge(s_ht, KD * n + k + 1)
                    act.activation(h_hi[:, k, :], htmp[:, k % 2, :], ACT.Copy).then_inc(s_hhi, 1)

            norm_hi(0)
            for i in range(2):
                for c in range(4):
                    u = 4 * i + c
                    act.wait_ge(s_used, u + 1)
                    if c < 2:
                        act.activation(cy[:, 2 * i + c, :], ps[:, c, :], ACT.Sigmoid).then_inc(s_take, 1)
                    else:
                        act.activation(glu[:, 2 * i + c - 2, PAD:PAD + SEQ], ps[:, c, :], ACT.Copy).then_inc(s_take, 1)
                    lead(u + 4)
            act.wait_ge(s_par, 4)
            act.wait_ge(s_ss0, TT)
            for u in range(8, 16):
                act.wait_ge(s_used, u + 1)
                act.activation(qk[:, u - 8, :], ps[:, u % 4, :], ACT.Copy).then_inc(s_take, 1)
                lead(u + 4)
                act.wait_ge(s_take, u + 1)
                act.activation(sqk[:, u - 8, :], qk[:, u - 8, :], ACT.Square).then_inc(s_qsq, 1)
            def value(t):
                if t < TT - 1:
                    act.wait_ge(s_vt, t + 1)
                else:
                    act.wait_ge(s_used, 20)
                act.activation(vtok[:, t, :], ps[:, t, :], ACT.Copy).then_inc(s_vc, 1)
            value(0)
            value(1)
            table(6)
            act.wait_ge(s_qv, 1)
            act.activation(nvar[:, 1, :], nvar[:, 0, :], ACT.Ln).then_inc(s_qr, 1)
            act.wait_ge(s_qr, 1)
            act.activation(nvar[:, 1, :], nvar[:, 1, :], ACT.Exp, scale=-0.5).then_inc(s_qr, 1)
            value(2)
            value(3)
            for u in range(U_OUT, U_OUT + 4):
                lead(u)

            for s in range(AH + 3):
                if s >= 3 and (s - 3) % 2 == 1:
                    j = (s - 3) // 2
                    act.wait_ge(s_pv, 2 * j + 2)
                    act.activation(h_hi[:, j, :], ps[:, 6, :], ACT.Copy).then_inc(s_mhi, 1)
                if s == 2:
                    act.wait_ge(s_mean, 1)
                    act.activation(sq[:, 1, :], ps[:, 7, :], ACT.Copy).then_inc(s_lc, 1)
                if s == 6:
                    act.wait_ge(s_rb, 2)
                    act.activation(sq[:, 1, :], ps[:, 7, :], ACT.Copy).then_inc(s_lc, 1)
                if s < AH:
                    z = zl[:, s % 3, :]
                    act.wait_ge(s_z, s + 1)
                    if s >= 3:
                        act.wait_ge(s_pv, s - 2)
                    act.activation(z, zps(s), ACT.Abs).then_inc(s_ab, 1)
                    act.wait_ge(s_ab, 2 * s + 1)
                    act.activation(z, z, ACT.Exp, scale=-1.0).then_inc(s_ab, 1)
                    act.wait_ge(s_ab, 2 * s + 2)
                    act.activation(z, z, ACT.Ln, bias=1.0).then_inc(s_l, 1)
                if 1 <= s <= AH:
                    act.wait_ge(s_dm, 2 * s)
                    act.activation(zl[:, (s - 1) % 3, :], zps(s - 1), ACT.Exp).then_inc(s_w, 1)
                if s == 7:
                    for c in range(CT):
                        act.wait_ge(s_ly, c + 1)
                        act.activation(cy[:, c, :], cy[:, c, :], ACT.Silu, scale=par[:, 0, C_LG + c:C_LG + c + 1],
                                       bias=par[:, 0, C_LB + c:C_LB + c + 1]).then_inc(s_ls, 1)
                    for c in range(CT):
                        act.wait_ge(s_ls, c + 1)
                        act.activation(h_hi[:, CT + c, :], cy[:, c, :], ACT.Copy).then_inc(s_mhi, 1)
                    table(6)

            def squares(n, m):
                act.wait_ge(s_x, 8 * (n - 1) + m + 1)
                if m < 3:
                    act.wait_ge(s_stat, STATS[n])
                else:
                    act.wait_ge(s_acc, 5 * (n - 1) + m - 2)
                act.activation(sq[:, m % 2, :] if m else htmp[:, 0, :], xT[:, m, :], ACT.Square).then_inc(s_sq, 1)

            def projected(n, u0):
                for m in range(KD):
                    if m < KD - 1:
                        lead(u0 + m)
                    squares(n, m)
                lead(u0 + KD - 1)

            projected(1, U_OUT + 4)
            norm_hi(1)

            def ffn(lay, u0, wcol, bcol):
                def quad(i, leads, wait=True):
                    j0 = KF * lay + 2 * i
                    def tap0(c):
                        act.activation(cv[:, c, :], ps[:, c, :], ACT.Identity,
                                       scale=par[:, 1 + lay, bass.ds(2 * KF + 2 * i + c, 1)],
                                       bias=par[:, 0, bass.ds(bcol + 2 * i + c, 1)]).then_inc(s_t0, 1)
                    def silu(c):
                        act.wait_ge(s_conv, j0 + c + 1)
                        act.activation(cv[:, c, :], cv[:, c, :], ACT.Silu).then_inc(s_silu, 1)
                    def hi(c):
                        act.wait_ge(s_gv, j0 + c + 1)
                        act.activation(a_hi[:, bass.ds(2 * i + c, 1), :].rearrange("p a n -> p (a n)"),
                                       cv[:, c, :], ACT.Copy).then_inc(s_ahi, 1)
                    for c in range(4):
                        act.wait_ge(s_used, u0 + 4 * i + c + 1)
                        if c < 2:
                            if wait:
                                act.wait_ge(s_alo, j0 + c - 1)
                            tap0(c)
                        leads(c)
                        if c >= 1 and c < 3:
                            silu(c - 1)
                        if c == 3:
                            hi(0)
                    hi(1)
                quad(0, lambda c: lead(u0 + 4 + c), wait=lay > 0)
                with act.Fori(1, NUP - 1) as i:
                    quad(i, lambda c: lead(u0 + 4 + c, i))
                quad(NUP - 1, lambda c: lead(u0 + 4 * NUP + c))

            def final_gain(m):
                act.wait_ge(s_sq, 8 * 3 + m + 1)
                act.activation(xT[:, m, :], xT[:, m, :], ACT.Copy, scale=par[:, 0, C_FN + m:C_FN + m + 1]).then_inc(s_gx, 1)

            def down(n, u0, more):
                with act.Fori(0, 4) as i:
                    for c in range(4):
                        act.wait_ge(s_used, u0 + 4 * i + c + 1)
                        lead(u0 + 4 + c, i)
                for c in range(16, KF - 2):
                    if c < KF - 4 or more:
                        lead(u0 + c + 4)
                for m in range(KD):
                    squares(n, m)
                    if n == 4 and m:
                        final_gain(m - 1)
                if more:
                    lead(u0 + KF + 2)
                    lead(u0 + KF + 3)

            ffn(0, U_UP, 1, C_FB)
            down(2, U_DOWN, True)
            norm_hi(2)

            def bias(c):
                return par[:, 0, C_BA + c:C_BA + c + 1]

            def take(n, out_ap, in_ap, func=ACT.Copy, **kw):
                act.wait_ge(s_used, U_IN2 + n + 1)
                act.activation(out_ap, in_ap, func, **kw).then_inc(s_take2, 1)

            take(0, kT[:, 0, :], ps[:, 2, :], ACT.Identity, bias=bias(4))
            take(1, vT[:], ps[:, 3, :], ACT.Identity, bias=bias(5))
            act.wait_ge(s_take2, 1)
            for half in range(2):
                act.dma_start(kT[64 * half:64 * half + 64, 1, :],
                              kT[64 - 64 * half:128 - 64 * half, 0, :]).then_inc(s_ks, 16)
            lead(U_IN2 + 4)
            lead(U_IN2 + 5)
            for c in range(4):
                take(2 + c, aq[:, c, :], ps[:, c, :], ACT.Identity, bias=bias(c))
                lead(U_IN2 + 6 + c)
                if c == 1:
                    act.wait_ge(s_vtp, 1)
                    act.activation(vt2[:].rearrange("p t n -> p (t n)"), ps[:, 6, :], ACT.Copy).then_inc(s_vt2, 1)
            table(6)
            act.wait_ge(s_lb, 3)
            act.activation(lbt[:, 1:3, :], lbt[:, 1:3, :], ACT.Exp).then_inc(s_lb, 1)

            def o_hi(n):
                b, g = n // 2, n % 2
                act.wait_ge(s_po, n + 1)
                act.activation(m_hi[:, 2 * g:2 * g + 2, b * P:(b + 1) * P],
                               ps[:, 6, 0:2 * P].rearrange("p (j q) -> p j q", j=2), ACT.Copy).then_inc(s_ohi, 1)

            def exponentials(n):
                p, w = sm[:, n % 2], smx[:, n % 2]
                lo = P if n < 2 else 0
                act.wait_ge(s_mx, 4 * n + 4)
                for a in range(4):
                    act.activation(p[:, a, lo:], p[:, a, lo:], ACT.Exp, bias=w[:, 1, a:a + 1],
                                   accum_out=w[:, 3, a:a + 1]).then_inc(s_pe, 1)
                act.activation(w[:, 2, :], w[:, 2, :], ACT.Exp).then_inc(s_pe, 1)

            exponentials(0)
            for n in range(8):
                if n >= 1:
                    o_hi(n - 1)
                if n < 7:
                    exponentials(n + 1)
                if n < 4:
                    take(6 + n, kk[:, n, :], ps[:, n, :])
                else:
                    take(6 + n, qq[:, n - 4, :], ps[:, n - 4, :], scale=float(P) ** -0.5)
                lead(U_IN2 + 10 + n)
                for half in range(1 if n < 2 else 0, 2):
                    act.wait_ge(s_tr, n + 1)
                    if n >= 2:
                        act.wait_ge(s_po, n - 1)
                    act.activation(pT[:, n % 2, half, :], ps[:, 6 + half, :], ACT.Copy).then_inc(s_pT, 1)
                if n == 5:
                    act.wait_ge(s_take2, 10)
                    for j in range(4):
                        act.activation(kk[:, j, :], kk[:, j, :], ACT.Sigmoid).then_inc(s_lf, 1)
                    table(6)
            o_hi(7)
            for j in range(4):
                act.wait_ge(s_f, 2 * j + 2)
                act.activation(bb[:, j, :], bb[:, j, :], ACT.Ln).then_inc(s_lf, 1)

            def between(j):
                act.wait_ge(s_of, j + 1)
                act.activation(kd[:, j % 2], kd[:, j % 2], ACT.Exp).then_inc(s_ofe, 1)
                if j:
                    act.wait_ge(s_ofk, 6 * j)
                act.activation(eb[:], chunks(bb[:, j, :])[:, 1:4, :], ACT.Exp).then_inc(s_ofe, 1)

            def after(i):
                j, lv = i // 8, i % 8
                if lv == 2:
                    act.wait_ge(s_pvh, j + 1)
                    if j >= 2:
                        act.wait_ge(s_yn, j - 1)
                    act.activation(htmp[:, j % 2, :], ps[:, 6, :], ACT.Copy).then_inc(s_oc, 1)
                    act.wait_ge(s_oc, 2 * j + 1)
                    act.activation(sq[:, j % 2, :], htmp[:, j % 2, :], ACT.Square).then_inc(s_oc, 1)

            def copy_between(j):
                act.wait_ge(s_ofp, j + 1)
                if j >= 2:
                    act.wait_ge(s_pvh, j - 1)
                act.activation(off[:, j % 2, 0:4, :].rearrange("p c n -> p (c n)"), ps[:, 6, :], ACT.Copy).then_inc(s_ofc, 1)
                act.activation(off[:, j % 2, 4:6, :].rearrange("p c n -> p (c n)"), ps[:, 7, 0:2 * P], ACT.Copy).then_inc(s_ofc, 1)

            for i in range(32):
                j, lv = i // 8, i % 8
                if lv == 0 and j:
                    copy_between(j - 1)
                if lv == 0:
                    between(j)
                if lv:
                    act.wait_ge(s_dif, 7 * j + lv)
                    act.activation(ee[:, i % 3, :], ee[:, i % 3, :], ACT.Exp).then_inc(s_e, 1)
                if j:
                    after(i - 8)
                if i in FILL:
                    t = FILL.index(i)
                    if t < 3:
                        act.wait_ge(s_vh, t + 1)
                        act.activation(vh[:, t, :], ps[:, t, :], ACT.Copy).then_inc(s_take2, 1)
                    elif t == 3:
                        act.wait_ge(s_used, U_IN2 + 18)
                        act.activation(vh[:, t, :], ps[:, t, :], ACT.Copy).then_inc(s_take2, 1)
                        for c in range(4):
                            lead(U_IN2 + 18 + c)
                    else:
                        take(14 + t, aq[:, t - 4, :], ps[:, t - 4, :])
                        lead(U_OUT2 + t - 4)
            copy_between(3)
            act.wait_ge(s_take2, 22)
            for j in range(4):
                act.activation(aq[:, j, :], aq[:, j, :], ACT.Silu).then_inc(s_gsil, 1)
            after(26)
            for j in range(4):
                act.wait_ge(s_g2, j + 1)
                act.activation(h_hi[:, j, :], kk[:, j, :], ACT.Copy).then_inc(s_g2hi, 1)

            projected(3, U_OUT2 + 4)
            norm_hi(3)
            ffn(1, U_UP2, 2, C_FB2)
            down(4, U_DOWN2, False)
            final_gain(KD - 1)
            act.wait_ge(s_rstd, 10)
            for n in range(1, 8, 2):
                t, half, bank = OUT_TILES[n]
                act.wait_ge(s_ft, n + 1)
                act.activation(obuf[:, n, :], ps[:, bank, :], ACT.Copy, scale=rstd[:, t:t + 1]).then_inc(s_fin2, 1)

        @block.vector
        def _(dve):
            counts = {}
            def link(ins, s, base=0):
                counts[s] = counts.get(s, base) + 1
                ins.then_inc(s, 1)
                dve.wait_ge(s, counts[s])

            dve.wait_ge(s_const, 16)
            dve.tensor_copy(ntri[:], ntri_f[:]).then_inc(s_cdve, 1)
            dve.tensor_scalar(nones[:], ones[:], -1.0, None, ALU.mult).then_inc(s_cdve, 1)
            for m in range(KD):
                dve.wait_ge(s_xp, m + 1)
                dve.tensor_copy(xT[:, m, :], ps[:, 4 + m % 4, :]).then_inc(s_xT, 1)
            for t, n in enumerate(PROWS):
                dve.wait_ge(s_pp, t + 1)
                dve.tensor_copy(par[:, t, 0:n], ps[:, t, 0:n]).then_inc(s_par, 1)
            dve.wait_ge(s_par, 4)
            dve.tensor_scalar(gq8[:], par[:, 0, C_QG:C_QG + 1], 0.125, None, ALU.mult).then_inc(s_cdve, 1)

            def spread(n):
                dve.wait_ge(s_rstd, n)
                dve.tensor_tensor(diag[:], ident[:, None, :].to_broadcast([P, TT, P]),
                                  rstd[:, :, None].to_broadcast([P, TT, P]), ALU.mult).then_inc(s_diag, 1)

            def variance(src, div):
                dve.tensor_scalar(stat[:], src, 1.0 / div, EPS, ALU.mult, ALU.add).then_inc(s_var, 1)

            def normalize(n, rb_n, gcol, bank):
                def rest(k):
                    dve.wait_ge(s_hhi, KD * n + k + 1)
                    dve.tensor_tensor(h_lo[:, k, :], htmp[:, k % 2, :], h_hi[:, k, :].bitcast(F32),
                                      ALU.subtract).then_inc(s_hlo, 1)
                dve.wait_ge(s_rb, rb_n)
                for k in range(KD):
                    if k >= 2:
                        dve.wait_ge(s_hlo, KD * n + k - 1)
                    dve.scalar_tensor_tensor(htmp[:, k % 2, :], xT[:, k, :], par[:, 0, gcol + k:gcol + k + 1],
                                             ps[:, bank, :], ALU.mult, ALU.mult).then_inc(s_ht, 1)
                    if k >= 1:
                        rest(k - 1)
                rest(KD - 1)

            dve.wait_ge(s_ss0, TT)
            variance(ss0[:], DM)
            spread(1)
            dve.wait_ge(s_xT, KD)
            normalize(0, 1, C_N1, 5)

            for i in range(2):
                dve.wait_ge(s_take, 8 * i // 2 + 4)
                for c in range(2):
                    j = 2 * i + c
                    dve.tensor_tensor(glu[:, j, PAD:PAD + SEQ], glu[:, j, PAD:PAD + SEQ], cy[:, j, :],
                                      ALU.mult).then_inc(s_glu, 1)
                dve.wait_ge(s_glu, 2 * i + 2)
                t0 = 2 * CK * i
                for c in range(2):
                    j = 2 * i + c
                    dve.tensor_scalar(cy[:, j, :], glu[:, j, 0:SEQ], par[:, 3, j:j + 1],
                                      par[:, 0, C_CB + j:C_CB + j + 1], ALU.mult, ALU.add).then_inc(s_tap, 1)
                with dve.Fori(0, PAD // 5) as n:
                    for r in range(5):
                        for c in range(2):
                            j = 2 * i + c
                            dve.wait_ge(s_tap, t0 + 10 * n + 2 * r + c + 1)
                            dve.scalar_tensor_tensor(
                                cy[:, j, :], glu[:, j, bass.ds(5 * n + r + 1, SEQ)],
                                par[:, 3, bass.ds(20 * n + 4 * r + 4 + j, 1)], cy[:, j, :],
                                ALU.mult, ALU.add).then_inc(s_tap, 1)

            dve.wait_ge(s_qst, 1)
            link(dve.tensor_scalar(nvar[:, 0, :], ps[0:16, 4, :], 1.0 / 64, EPS, ALU.mult, ALU.add), s_qv)
            dve.wait_ge(s_qr, 2)
            link(dve.tensor_tensor(nvar[:, 2, :], nvar[:, 1, :], nvar[:, 1, :], ALU.mult), s_qv)
            link(dve.tensor_tensor(nvar[:, 2, :], nvar[:, 2, :], nvar[:, 0, :], ALU.mult), s_qv)
            link(dve.tensor_scalar(nvar[:, 2, :], nvar[:, 2, :], -0.5, 1.5, ALU.mult, ALU.add), s_qv)
            link(dve.tensor_tensor(nvar[:, 1, :], nvar[:, 1, :], nvar[:, 2, :], ALU.mult), s_qv)
            dve.wait_ge(s_cdve, 3)
            for j in range(8):
                g = gq8[:, 0:1] if j < 4 else par[:, 0, C_KG:C_KG + 1]
                dve.wait_ge(s_qb, j + 1)
                dve.scalar_tensor_tensor(qk[:, j, :], qk[:, j, :], g, ps[:, 4 + j % 4, :],
                                         ALU.mult, ALU.mult).then_inc(s_qn, 1)

            def blocks(t):
                return t.rearrange("p (a n) -> p a n", n=P)[:, 0:9:4, :], t[:, ZOFF[1]:ZOFF[1] + P]

            for s in range(AH + 3):
                if s >= 3 and (s - 3) % 2 == 1:
                    j = (s - 3) // 2
                    dve.wait_ge(s_mhi, j + 1 + (CT if j >= 2 else 0))
                    dve.tensor_tensor(h_lo[:, j, :], ps[:, 6, :], h_hi[:, j, :].bitcast(F32),
                                      ALU.subtract).then_inc(s_mlo, 1)
                if 1 <= s <= AH:
                    dve.wait_ge(s_tail, s)
                    three, one = blocks(zps(s - 1))
                    dve.scalar_tensor_tensor(three, three, 0.0, nmask[:, None, :].to_broadcast([P, 3, P]),
                                             ALU.min, ALU.add).then_inc(s_dm, 1)
                    dve.scalar_tensor_tensor(one, one, 0.0, nmask[:], ALU.min, ALU.add).then_inc(s_dm, 1)
                if s == 4:
                    dve.wait_ge(s_stat, 1)
                    variance(ps[:, 7, 0:TT], CT * P)
                if s < AH:
                    z = zl[:, s % 3, :]
                    dve.wait_ge(s_l, s + 1)
                    link(dve.scalar_tensor_tensor(z, zps(s), 0.0, z, ALU.max, ALU.add), s_sp)
                    three, one = blocks(z)
                    dve.tensor_tensor(three, three, smask[:, None, :].to_broadcast([P, 3, P]), ALU.mult).then_inc(s_sp, 1)
                    counts[s_sp] += 1
                    link(dve.tensor_tensor(one, one, smask[:], ALU.mult), s_sp)
                    if s >= 2:
                        dve.wait_ge(s_tail, s - 1)
                    link(dve.tensor_copy(sp_hi[:, s % 2, :], z), s_sp)
                    dve.tensor_tensor(sp_lo[:, s % 2, :], z, sp_hi[:, s % 2, :].bitcast(F32),
                                      ALU.subtract).then_inc(s_spl, 1)
                if s == 4:
                    spread(2)

            def residual(m, bank, sem, value):
                dve.wait_ge(sem, value)
                dve.tensor_tensor(xT[:, m, :], xT[:, m, :], ps[:, bank, :], ALU.add).then_inc(s_x, 1)

            def norm(n, rb_n, gcol):
                dve.wait_ge(s_stat, STATS[n] + 3)
                variance(ps[:, 4, 0:TT], DM)
                if gcol is not None:
                    spread(rb_n)
                    normalize(n, rb_n, gcol, 5)

            for m in range(KD):
                residual(m, OUT_BANK[m], s_used, U_OUT + m + 1)
            norm(1, 3, C_N2)

            def ffn(lay):
                def quad(i):
                    j0 = KF * lay + 2 * i
                    for c in range(2):
                        w = 1 + lay
                        dve.wait_ge(s_t0, j0 + c + 1)
                        dve.scalar_tensor_tensor(cv[:, c, 1:], ps[:, c, 0:SEQ - 1],
                                                 par[:, w, bass.ds(KF + 2 * i + c, 1)], cv[:, c, 1:],
                                                 ALU.mult, ALU.add).then_inc(s_tp, 1)
                        dve.wait_ge(s_tp, j0 + c + 1)
                        dve.scalar_tensor_tensor(cv[:, c, 2:], ps[:, c, 0:SEQ - 2],
                                                 par[:, w, bass.ds(2 * i + c, 1)], cv[:, c, 2:],
                                                 ALU.mult, ALU.add).then_inc(s_conv, 1)
                    for c in range(2):
                        dve.wait_ge(s_silu, j0 + c + 1)
                        dve.wait_ge(s_used, (U_UP2 if lay else U_UP) + 4 * i + 3 + c)
                        dve.tensor_tensor(cv[:, c, :], cv[:, c, :], ps[:, 2 + c, :], ALU.mult).then_inc(s_gv, 1)
                    for c in range(2):
                        dve.wait_ge(s_ahi, j0 + c + 1)
                        dve.tensor_tensor(a_lo[:, bass.ds(2 * i + c, 1), :].rearrange("p a n -> p (a n)"),
                                          cv[:, c, :],
                                          a_hi[:, bass.ds(2 * i + c, 1), :].rearrange("p a n -> p (a n)").bitcast(F32),
                                          ALU.subtract).then_inc(s_alo, 1)
                with dve.Fori(0, NUP) as i:
                    quad(i)

            def down(lay, end):
                for m in range(KD - 1):
                    residual(m, (m + 4) % 8, s_out, (KD - 1) * lay + m + 1)
                residual(KD - 1, 3, s_used, end)

            ffn(0)
            down(0, U_IN2)
            norm(2, 4, C_NM)

            l0, l1 = (par[:, 0, C_LL + 4 * r:C_LL + 4 * r + 4] for r in range(2))
            dve.wait_ge(s_par, 1)
            link(dve.tensor_tensor(lbt[:, 0, :], l0, l1, ALU.max), s_lb)
            link(dve.tensor_tensor(lbt[:, 1, :], l0, lbt[:, 0, :], ALU.subtract), s_lb)
            link(dve.tensor_tensor(lbt[:, 2, :], l1, lbt[:, 0, :], ALU.subtract), s_lb)
            def o_lo(n):
                b, g = n // 2, n % 2
                dve.wait_ge(s_ohi, n + 1)
                dve.tensor_tensor(m_lo[:, 2 * g:2 * g + 2, b * P:(b + 1) * P],
                                  ps[:, 6, 0:2 * P].rearrange("p (j q) -> p j q", j=2),
                                  m_hi[:, 2 * g:2 * g + 2, b * P:(b + 1) * P].bitcast(F32),
                                  ALU.subtract).then_inc(s_olo, 1)

            def pairs(t):
                return t.rearrange("p (h j) -> p h j", h=2)

            dve.wait_ge(s_gc, GC)
            dve.wait_ge(s_sink, 16)
            def maxima(n):
                g = n % 2
                p, w = sm[:, n % 2], smx[:, n % 2]
                lo = P if n < 2 else 0
                dve.wait_ge(s_sc, n + 1)
                if n >= 2:
                    dve.wait_ge(s_tr, n - 1)
                src = ps[:, 4:6, :].rearrange("p b (a k) -> p (b a) k", k=2 * P)
                sink = sinkb[:, 4 * g:4 * g + 4].rearrange("p (j h) -> p h j", h=2)
                dve.scalar_tensor_tensor(p[:, :, lo:], src[:, :, lo:], 0.125,
                                         band[:, None, lo:].to_broadcast([P, 4, 2 * P - lo]),
                                         ALU.mult, ALU.add).then_inc(s_sm, 1)
                dve.wait_ge(s_sm, n + 1)
                link(dve.tensor_reduce(w[:, 0, :], p[:, :, lo:], AX.X, ALU.max), s_mx)
                link(dve.tensor_tensor(pairs(w[:, 0, :]), pairs(w[:, 0, :]), sink, ALU.max), s_mx)
                dve.tensor_scalar(w[:, 1, :], w[:, 0, :], -1.0, None, ALU.mult).then_inc(s_mx, 1)
                counts[s_mx] += 1
                link(dve.tensor_tensor(pairs(w[:, 2, :]), sink, pairs(w[:, 0, :]), ALU.subtract), s_mx)

            maxima(0)
            for n in range(8):
                p, w = sm[:, n % 2], smx[:, n % 2]
                lo = P if n < 2 else 0
                dve.wait_ge(s_pe, 5 * n + 5)
                link(dve.tensor_tensor(w[:, 4, :], w[:, 3, :], w[:, 2, :], ALU.add), s_den)
                link(dve.reciprocal(w[:, 5, :], w[:, 4, :]), s_den)
                dve.tensor_tensor(p[:, :, lo:], p[:, :, lo:],
                                  w[:, 5, :, None].to_broadcast([P, 4, 2 * P - lo]), ALU.mult).then_inc(s_p, 1)
                if n < 7:
                    maxima(n + 1)
                if n >= 1:
                    o_lo(n - 1)
            dve.wait_ge(s_lb, 4)
            counts[s_lb] = 4
            link(dve.tensor_tensor(lbt[:, 0, :], lbt[:, 1, :], lbt[:, 2, :], ALU.add), s_lb)
            link(dve.reciprocal(lbt[:, 0, :], lbt[:, 0, :]), s_lb)
            link(dve.tensor_tensor(lbt[:, 3, :], lbt[:, 1, :], lbt[:, 0, :], ALU.mult), s_lb)
            link(dve.tensor_scalar(lbt[:, 4, :], lbt[:, 3, :], -1.0, 1.0, ALU.mult, ALU.add), s_lb)
            for j in range(4):
                dve.wait_ge(s_lf, j + 1)
                link(dve.tensor_scalar(bb[:, j, :], kk[:, j, :], lbt[:, 4, j:j + 1], lbt[:, 3, j:j + 1],
                                       ALU.mult, ALU.add), s_f)
                dve.tensor_scalar(kk[:, j, :], bb[:, j, :], -1.0, 1.0, ALU.mult, ALU.add).then_inc(s_f, 1)
                counts[s_f] += 1
            o_lo(7)
            for j in range(4):
                dve.wait_ge(s_lf, 4 + j + 1)
                link(dve.tensor_tensor_scan(bb[:, j, :], cmask[:], bb[:, j, :], 0.0, ALU.mult, ALU.add), s_b)

            def exponents(i):
                j, m = i // 8, 1 << (i % 8 - 1)
                b, e = halves(bb[:, j, :], m), halves(ee[:, i % 3, :], m)
                middle = b[:, :, 0, m - 1:m].to_broadcast([P, SEQ // (2 * m), m])
                if i >= 3:
                    dve.wait_ge(s_lv, i - 2)
                dve.tensor_tensor(e[:, :, 0, :], middle, b[:, :, 0, :], ALU.subtract)
                dve.tensor_tensor(e[:, :, 1, :], b[:, :, 1, :], middle, ALU.subtract).then_inc(s_dif, 1)

            def times_keys(i):
                j, m = i // 8, 1 << (i % 8 - 1)
                dve.wait_ge(s_e, 7 * j + i % 8)
                low = halves(ee[:, i % 3, :], m)[:, :, 0, :]
                dve.tensor_tensor(low, low, halves(kk[:, j, :], m)[:, :, 0, :], ALU.mult).then_inc(s_ek, 1)

            def collect(i):
                j, lv = i // 8, i % 8
                dve.wait_ge(s_lv, i + 1)
                if lv == 0 and j >= 2:
                    dve.wait_ge(s_pvh, j - 1)
                if lv:
                    dve.wait_ge(s_cp, i)
                d = acc[:, j % 2]
                src = chunks(ps[:, 4 + i % 2, :])
                if lv == 0:
                    dve.tensor_tensor(d, src, ident[:, None, :].to_broadcast([P, TT, P]), ALU.mult).then_inc(s_cp, 1)
                else:
                    dve.copy_predicated(d, lmask[:, lv - 1:lv, :].to_broadcast([P, TT, P]), src).then_inc(s_cp, 1)

            def decays(j):
                b = chunks(bb[:, j, :])
                if j >= 2:
                    dve.wait_ge(s_ofp, j - 1)
                dve.tensor_tensor(kd[:, j % 2], b[:, 0:3, P - 1:P].to_broadcast([P, 3, P]), b[:, 0:3, :],
                                  ALU.subtract).then_inc(s_of, 1)

            def between(j):
                k, q = chunks(kk[:, j, :]), chunks(qq[:, j, :])
                dve.wait_ge(s_ofe, 2 * j + 2)
                if j:
                    dve.wait_ge(s_ofp, j)
                for at, c in ((0, 0), (3, 1), (5, 2)):
                    dve.tensor_tensor(qs[:, at, :], q[:, c + 1, :], eb[:, c, :], ALU.mult).then_inc(s_ofk, 1)
                dve.tensor_tensor(kd[:, j % 2], kd[:, j % 2], k[:, 0:3, :], ALU.mult)

            def between2(j):
                dve.wait_ge(s_ofk, 6 * j + 3)
                dve.tensor_scalar(qs[:, 4, :], qs[:, 5, :], eb[:, 1, P - 1:P], None, ALU.mult).then_inc(s_ofk, 1)
                dve.tensor_scalar(qs[:, 1, :], qs[:, 3, :], eb[:, 0, P - 1:P], None, ALU.mult).then_inc(s_ofk, 1)
                dve.wait_ge(s_ofk, 6 * j + 5)
                dve.tensor_scalar(qs[:, 2, :], qs[:, 4, :], eb[:, 0, P - 1:P], None, ALU.mult).then_inc(s_ofk, 1)

            def after(i):
                j, lv = i // 8, i % 8
                if lv == 4:
                    dve.wait_ge(s_stat, STATS[2] + 3 + j + 1)
                    variance(ps[:, 7, 0:TT], P)
                if lv == 5:
                    spread(5 + j)
                if lv == 7:
                    dve.wait_ge(s_rb, 5 + j)
                    dve.scalar_tensor_tensor(kk[:, j, :], htmp[:, j % 2, :], par[:, 0, C_HG:C_HG + 1],
                                             ps[:, 7, :], ALU.mult, ALU.mult).then_inc(s_yn, 1)

            dve.wait_ge(s_po, 8)
            for i in range(34):
                if i < 32 and i % 8:
                    exponents(i)
                if 1 <= i < 33 and (i - 1) % 8:
                    times_keys(i - 1)
                if i >= 2:
                    collect(i - 2)
                if i < 32:
                    if i % 8 == 0:
                        decays(i // 8)
                    if i % 8 == 1:
                        between(i // 8)
                    if i % 8 == 2:
                        between2(i // 8)
                if 8 <= i < 32:
                    after(i - 8)
            def gated(j):
                dve.wait_ge(s_gsil, j + 1)
                dve.wait_ge(s_yn, j + 1)
                dve.tensor_tensor(kk[:, j, :], kk[:, j, :], aq[:, j, :], ALU.mult).then_inc(s_g2, 1)

            def gated_lo(j):
                dve.wait_ge(s_g2hi, j + 1)
                dve.tensor_tensor(h_lo[:, j, :], kk[:, j, :], h_hi[:, j, :].bitcast(F32),
                                  ALU.subtract).then_inc(s_g2lo, 1)

            for j in range(3):
                gated(j)
            for j in range(3):
                gated_lo(j)
            after(28)
            after(29)
            after(31)
            gated(3)
            gated_lo(3)

            for m in range(KD):
                residual(m, m % 4, s_used, U_OUT2 + m + 1)
            norm(3, 9, C_NF)
            ffn(1)
            down(1, U_END)
            norm(4, 10, None)
            dve.wait_ge(s_rstd, 10)
            for n in range(0, 8, 2):
                t, half, bank = OUT_TILES[n]
                dve.wait_ge(s_ft, n + 1)
                dve.tensor_scalar(obuf[:, n, :], ps[:, bank, :], rstd[:, t:t + 1], None,
                                  ALU.mult).then_inc(s_fin, 1)

        @block.tensor
        def _(pe):
            def unit_mms(bank, at, k, first, last, hi=h_hi, lo=h_lo, used=False):
                whi, wlo = (unit_view(w, at, False)[:, k, :] for w in (w_hi, w_lo))
                pe.matmul(ps[:, bank, :], whi, hi[:, k, :], start=first, stop=False, skip_group_check=True)
                pe.matmul(ps[:, bank, :], whi, lo[:, k, :], start=False, stop=False, skip_group_check=True)
                mm = pe.matmul(ps[:, bank, :], wlo, hi[:, k, :], start=False, stop=last, skip_group_check=True)
                if used:
                    mm.then_inc(s_used, 1)

            def unit(at, bank, i=0, order=range(KD)):
                pe.wait_ge(s_lo, at + 4 * i + 1)
                for n, k in enumerate(order):
                    unit_mms(bank, at, k, n == 0, n == KD - 1, used=(n == KD - 1))

            def pair_first(at, n, banks):
                pe.wait_ge(s_lo, at + 2)
                for k in range(KD):
                    pe.wait_ge(s_hlo, KD * n + k + 1)
                    for c in range(2):
                        unit_mms(banks[c], at + c, k, k == 0, k == KD - 1, used=(k == KD - 1))

            def first_quad(at, n, free):
                for c in range(2):
                    free(c)
                pair_first(at, n, (0, 1))
                for c in (2, 3):
                    free(c)
                    unit(at + c, c)

            pe.wait_ge(s_const, 4)
            for m in range(KD):
                if m >= 4:
                    pe.wait_ge(s_xT, m - 3)
                for t in range(TT):
                    if m == 0 and t % 2 == 0:
                        pe.wait_ge(s_xin[t // 2], 16)
                    mm = pe.transpose(ps[:, 4 + m % 4, t * P:(t + 1) * P], xtok[:, t, m * P:(m + 1) * P], ident[:])
                mm.then_inc(s_xp, 1)
            pe.wait_ge(s_prow, 16 * NPROW)
            for t, n in enumerate(PROWS):
                pe.transpose(ps[:, t, 0:n], prow[0:n, t, :], ident[0:n, 0:n]).then_inc(s_pp, 1)

            def spread(n, bank):
                pe.wait_ge(s_diag, n)
                pe.matmul(ps[:, bank, :], ones[:], diag[:].rearrange("p t n -> p (t n)"),
                          start=True, stop=True, skip_group_check=True).then_inc(s_rb, 1)

            pe.wait_ge(s_xT, KD)
            spread(1, 5)
            pe.wait_ge(s_par, 4)
            first_quad(U_IN, 0, lambda c: None)
            with pe.Fori(1, 4) as i:
                for c in range(4):
                    pe.wait_ge(s_take, 4 * i + c - 3)
                    unit(U_IN + c, c, i)

            def values(t, done, ks=range(KD)):
                for k in ks:
                    for n, (a, w) in enumerate(((h_hi, w_hi), (h_lo, w_hi), (h_hi, w_lo))):
                        rhs = w[:, :, k * P:(k + 1) * P]
                        mm = pe.matmul(ps[:, t, :].rearrange("p (s n) -> p s n", n=P), a[:, k, t * P:(t + 1) * P], rhs,
                                       start=(k == 0 and n == 0), stop=(k == KD - 1 and n == 2), skip_group_check=True)
                if ks[-1] == KD - 1:
                    mm.then_inc(done, 1) if t < TT - 1 else mm.then_inc(s_used, 4)

            pe.wait_ge(s_ht, KD)
            for j in range(8):
                pe.wait_ge(s_qsq, j + 1)
                mm = pe.matmul(ps[0:16, 4, :], sel[:, j, :], sqk[:, j, :], start=(j == 0), stop=(j == 7))
            mm.then_inc(s_qst, 1)
            pe.wait_ge(s_lo, 20)
            for t in range(TT):
                pe.wait_ge(s_take, 12 + t + 1)
                values(t, s_vt)
            pe.wait_ge(s_qv, 5)
            for j in range(8):
                if j >= 4:
                    pe.wait_ge(s_qn, j - 3)
                pe.matmul(ps[:, 4 + j % 4, :], selT[:, j, :], nvar[:, 1, :], start=True, stop=True).then_inc(s_qb, 1)
            pe.wait_ge(s_qn, 8)
            pe.wait_ge(s_vc, 4)

            def scores(h):
                j, lo = h // 2, 64 * (h % 2)
                if h >= 2:
                    pe.wait_ge(s_w, h - 1)
                for b in range(4):
                    mm = pe.matmul(zps(h)[:, ZOFF[b]:ZOFF[b] + ZLEN[b]], qk[lo:lo + 64, 4 + j, b * P:(b + 1) * P],
                                   qk[lo:lo + 64, j, b * P:SEQ], start=(b != 3), stop=False, skip_group_check=True)
                mm.then_inc(s_z, 1)

            def tails(h):
                pe.wait_ge(s_spl, h + 1)
                for b in range(4):
                    for b2 in range(b, 4):
                        o = ZOFF[b] + P * (b2 - b)
                        for part in (sp_hi, sp_lo):
                            mm = pe.matmul(zps(h)[:, o:o + ZLEN[b2]], (ntri if b2 == b else nones)[:],
                                           part[:, h % 2, ZOFF[b2]:ZOFF[b2] + ZLEN[b2]],
                                           start=False, stop=False, skip_group_check=True)
                mm.then_inc(s_tail, 1)

            def outputs(h):
                j, lo = h // 2, 64 * (h % 2)
                pe.wait_ge(s_w, h + 1)
                if h >= 2 and h % 2 == 0:
                    pe.wait_ge(s_mlo, j)
                for b in range(4):
                    mm = pe.matmul(ps[lo:lo + 64, 6, b * P:SEQ], vtok[:, b, h * 64:(h + 1) * 64],
                                   zl[:, h % 3, ZOFF[b]:ZOFF[b] + ZLEN[b]], start=(b == 0), stop=(b == 3),
                                   skip_group_check=True)
                mm.then_inc(s_pv, 1)

            def sums(bank, src, start, done):
                for t in range(TT):
                    mm = pe.matmul(ps[:, bank, t:t + 1], src[:, t * P:(t + 1) * P], ones[:, 0:1],
                                   start=(start and t == 0), stop=done, skip_group_check=True)
                mm.then_inc(s_stat, 1)

            def convolution_part(m):
                pe.wait_ge(s_lo, U_OUT + m + 1)
                for k in range(4, KD):
                    unit_mms(OUT_BANK[m], U_OUT + m, k, k == 4, False)

            pe.wait_ge(s_cdve, 2)
            for s in range(AH + 2):
                if s < AH:
                    scores(s)
                if s == 1:
                    pe.wait_ge(s_ln, 3)
                    pe.matmul(ps[:, 7, :], lnone[:], sq[:, 0, :], start=True, stop=True,
                              skip_group_check=True).then_inc(s_mean, 1)
                if s == 5:
                    spread(2, 7)
                if 1 <= s <= AH:
                    tails(s - 1)
                if s == 3:
                    pe.wait_ge(s_ln, LN_STEPS)
                    sums(7, sq[:, 0, :], True, True)
                if s == 9:
                    convolution_part(2)
                if s >= 2:
                    outputs(s - 2)
                if s == 8:
                    pe.wait_ge(s_w, 7)
                    pe.wait_ge(s_clo, CT)
                    convolution_part(0)
                    convolution_part(1)
                if s == 9:
                    convolution_part(3)

            def stream_sums(n, m):
                if m == 5:
                    pe.wait_ge(s_acc, 5 * n)
                    sums(4, htmp[:, 0, :], True, False)
                else:
                    pe.wait_ge(s_sq, 8 * (n - 1) + m + 1)
                    sums(4, sq[:, m % 2, :], False, m == KD - 1)

            pe.wait_ge(s_w, AH)
            pe.wait_ge(s_mlo, 4)
            for m in range(KD):
                if m >= 4:
                    pe.wait_ge(s_x, m - 3)
                pe.wait_ge(s_lo, U_OUT + m + 1)
                order = (0, 1, 2, 3) if m < 4 else (4, 5, 6, 7, 0, 1, 2, 3)
                for k in order:
                    if m == KD - 1 and k == 1:
                        stream_sums(1, 5)
                    unit_mms(OUT_BANK[m], U_OUT + m, k, m >= 4 and k == 4, k == 3, used=(k == 3))
            stream_sums(1, 6)
            stream_sums(1, 7)
            spread(3, 5)

            def ffn(lay, u0, n):
                first_quad(u0, n, lambda c: pe.wait_ge(s_x, 16 * lay + 8))
                with pe.Fori(1, NUP) as i:
                    for c in range(4):
                        pe.wait_ge(s_conv if c < 2 else s_gv, KF * lay + 2 * i + c % 2 - 1)
                        unit(u0 + c, c, i)

            def down(lay, u0, n, m_done, between=lambda: None):
                def product(at, k, m, first=False):
                    hi, lo = (a[:, bass.ds(k, 1), :].rearrange("p a n -> p (a n)") for a in (a_hi, a_lo))
                    whi, wlo = (unit_view(w, at, True) for w in (w_hi, w_lo))
                    for w, a, st in ((whi, hi, first), (whi, lo, False), (wlo, hi, False)):
                        mm = pe.matmul(ps[:, (m + 4) % 8, :], w[:, m * P:(m + 1) * P], a, start=st, stop=False,
                                       skip_group_check=True)
                    return mm

                def ktile(at, k, i=0, first=False):
                    pe.wait_ge(s_lo, at + 4 * i + 1)
                    pe.wait_ge(s_alo, KF * lay + k + 1)
                    for m in range(KD):
                        if first and m == 4:
                            pe.wait_ge(s_conv, KF * (lay + 1))
                        if first and m == 6:
                            pe.wait_ge(s_gv, KF * (lay + 1))
                        mm = product(at, k, m, first)
                    mm.then_inc(s_used, 1)
                pe.wait_ge(s_ht, KD * (n + 1))
                for c in range(4):
                    ktile(u0 + c, c, first=(c == 0))
                with pe.Fori(1, 5) as i:
                    for c in range(4):
                        ktile(u0 + c, 4 * i + c, i)
                pe.wait_ge(s_lo, u0 + KF)
                pe.wait_ge(s_alo, KF * (lay + 1))
                for m in range(KD):
                    for k in (KF - 2, KF - 1):
                        mm = product(u0 + k, k, m)
                        if m == KD - 1:
                            mm.then_inc(s_used, 1)
                    if m < KD - 1:
                        mm.then_inc(s_out, 1)
                between()
                for m in (5, 6, 7):
                    stream_sums(m_done, m)

            ffn(0, U_UP, 1)
            down(0, U_DOWN, 1, 2)

            spread(4, 5)
            pe.wait_ge(s_x, 16)
            pair_first(U_IN2, 2, (2, 3))
            for c in range(4):
                if c >= 2:
                    pe.wait_ge(s_take2, c - 1)
                unit(U_IN2 + 2 + c, c)
                if c == 0:
                    pe.wait_ge(s_take2, 2)
                    for t in range(TT):
                        mm = pe.transpose(ps[:, 6, t * P:(t + 1) * P], vT[:, t * P:(t + 1) * P], ident[:])
                    mm.then_inc(s_vtp, 1)

            def sliding_scores(n):
                b, g = n // 2, n % 2
                if n:
                    pe.wait_ge(s_sm, n)
                for a in range(4):
                    half, tile = a % 2, 2 * g + a // 2
                    k0 = max(b - 1, 0) * P
                    kn = (b + 1) * P - k0
                    o = ps[:, 4 + half, (a // 2) * 2 * P:(a // 2 + 1) * 2 * P][:, 2 * P - kn:]
                    mm = pe.matmul(o, aq[64 * half:64 * half + 64, tile, b * P:(b + 1) * P],
                                   kT[64 * half:64 * half + 64, (half + g) % 2, k0:k0 + kn],
                                   start=(a < 2), stop=True, skip_group_check=True)
                mm.then_inc(s_sc, 1)

            def sliding_transposes(n):
                pe.wait_ge(s_p, n + 1)
                if n:
                    pe.wait_ge(s_olo, n)
                for half in range(1 if n < 2 else 0, 2):
                    for a in range(4):
                        mm = pe.transpose(ps[:, 6 + half, a * P:(a + 1) * P], sm[:, n % 2, a, half * P:(half + 1) * P], ident[:])
                mm.then_inc(s_tr, 1)

            def sliding_outputs(n):
                b, g = n // 2, n % 2
                pe.wait_ge(s_pT, n + 1 if n < 2 else 2 * n)
                first = 1 if n < 2 else 0
                for par2 in range(2):
                    for half in range(first, 2):
                        mm = pe.matmul(ps[64 * par2:64 * par2 + 64, 6, 0:2 * P],
                                       vt2[:, b - 1 + half, 64 * g:64 * g + 64],
                                       pT[:, n % 2, half, 2 * P * par2:2 * P * (par2 + 1)],
                                       start=(half == first), stop=(half == 1), skip_group_check=True)
                mm.then_inc(s_po, 1)

            pe.wait_ge(s_take2, 6)
            pe.wait_ge(s_ks, 32)
            pe.wait_ge(s_vt2, 1)
            sliding_scores(0)
            for n in range(8):
                if n < 7:
                    sliding_scores(n + 1)
                if n:
                    sliding_outputs(n - 1)
                pe.wait_ge(s_take2, n + 3)
                unit(U_IN2 + 6 + n, n % 4)
                sliding_transposes(n)
            sliding_outputs(7)

            def level(i):
                j, lv = i // 8, i % 8
                if i >= 2:
                    pe.wait_ge(s_cp, i - 1)
                if lv:
                    pe.wait_ge(s_ek, 7 * j + lv)
                    pe.wait_ge(s_eq, 7 * j + lv)
                    k = q = ee[:, i % 3, :]
                else:
                    pe.wait_ge(s_f, 2 * j + 2)
                    k, q = kk[:, j, :], qq[:, j, :]
                for c in range(TT):
                    mm = pe.matmul(ps[:, 4 + i % 2, c * P:(c + 1) * P], k[:, c * P:(c + 1) * P], q[:, c * P:(c + 1) * P],
                                   start=(c == 0), stop=True, skip_group_check=True)
                mm.then_inc(s_lv, 1)

            def between(j):
                pe.wait_ge(s_ofk, 6 * j + 6)
                if j:
                    pe.wait_ge(s_yn, j)
                else:
                    pe.wait_ge(s_olo, 8)
                for bank, c0, s_, at, n in ((6, 0, 0, 0, 3), (6, 3, 2, 5, 1), (7, 0, 1, 3, 2)):
                    mm = pe.matmul(ps[:, bank, c0 * P:(c0 + n) * P], kd[:, j % 2, s_, :],
                                   qs[:, at:at + n, :].rearrange("p c n -> p (c n)"),
                                   start=(c0 == 0), stop=True, skip_group_check=True)
                mm.then_inc(s_ofp, 1)

            OFF_AT = (0, 4, 3)

            def after(i):
                j, lv = i // 8, i % 8
                if lv == 1:
                    pe.wait_ge(s_ofc, 2 * j + 2)
                    pe.wait_ge(s_cp, 8 * j + 8)
                    pe.wait_ge(s_take2, 18)
                    for s_ in range(TT):
                        w = vh[:, s_, j * P:(j + 1) * P]
                        mm = pe.matmul(ps[:, 6, s_ * P:(s_ + 1) * P], w, acc[:, j % 2, s_, :],
                                       start=(s_ == 0), stop=False, skip_group_check=True)
                        n = TT - 1 - s_
                        if n:
                            pe.matmul(ps[:, 6, (s_ + 1) * P:], w,
                                      off[:, j % 2, OFF_AT[s_]:OFF_AT[s_] + n, :].rearrange("p c n -> p (c n)"),
                                      start=False, stop=False, skip_group_check=True)
                    mm.then_inc(s_pvh, 1)
                if lv == 3:
                    pe.wait_ge(s_oc, 2 * j + 2)
                    sums(7, sq[:, j % 2, :], True, True)
                if lv == 6:
                    spread(5 + j, 7)

            def unit2(m, ks, first, last):
                for k in ks:
                    t_hi, t_lo, at = (h_hi, h_lo, k) if k < 4 else (m_hi, m_lo, k - 4)
                    whi, wlo = (unit_view(w, U_OUT2 + m, False)[:, k, :] for w in (w_hi, w_lo))
                    for n, (w, a) in enumerate(((whi, t_hi), (whi, t_lo), (wlo, t_hi))):
                        mm = pe.matmul(ps[:, m % 4, :], w, a[:, at, :], start=(first and k == ks[0] and n == 0),
                                       stop=(last and k == ks[-1] and n == 2), skip_group_check=True)
                if last:
                    mm.then_inc(s_used, 1)

            def attention_part(m):
                pe.wait_ge(s_take2, 19 + m)
                pe.wait_ge(s_lo, U_OUT2 + m + 1)
                unit2(m, (4, 5, 6, 7), True, False)

            def fill(i):
                if i > FILL[-1]:
                    if i % 2 == 0:
                        attention_part((i - FILL[-1]) // 2)
                    return
                t = sum(i > end for end in FILL)
                start = FILL[t - 1] + 1 if t else 0
                k0 = sum(FILL_K[start:i])
                ks = range(k0, k0 + FILL_K[i])
                if t < 4:
                    if i == 0:
                        pe.wait_ge(s_lo, U_IN2 + 18)
                    pe.wait_ge(s_take2, 10 + t + 1)
                    values(t, s_vh, ks)
                else:
                    at = U_IN2 + 14 + t
                    pe.wait_ge(s_lo, at + 1)
                    pe.wait_ge(s_take2, 14 + t - 3)
                    for k in ks:
                        unit_mms(t - 4, at, k, k == 0, k == KD - 1, used=(k == KD - 1))

            for i in range(32):
                fill(i)
                if i >= 8:
                    after(i - 8)
                if i % 8 == 7:
                    between(i // 8)
                level(i)
            attention_part(2)
            after(25)
            attention_part(3)
            after(27)
            pe.wait_ge(s_g2lo, 3)
            for m in range(2):
                unit2(m, (0, 1, 2), False, False)
            after(30)
            for m in range(2, 4):
                unit2(m, (0, 1, 2), False, False)
            pe.wait_ge(s_g2lo, 4)
            for m in range(KD):
                if m < 4:
                    unit2(m, (3,), False, True)
                else:
                    pe.wait_ge(s_x, 16 + m - 3)
                    pe.wait_ge(s_lo, U_OUT2 + m + 1)
                    unit2(m, (4, 5, 6, 7, 0), True, False)
                    if m == KD - 1:
                        stream_sums(3, 5)
                    unit2(m, (1, 2, 3), False, True)
            stream_sums(3, 6)
            stream_sums(3, 7)
            spread(9, 5)
            ffn(1, U_UP2, 3)

            def result(n):
                t, half, bank = OUT_TILES[n]
                if bank == 4:
                    pe.wait_ge(s_var, 10)
                else:
                    pe.wait_ge(s_x, 24 + (bank - 4) % 8 + 1)
                for f in range(4):
                    m = 4 * half + f
                    pe.wait_ge(s_gx, m + 1)
                    mm = pe.transpose(ps[:, bank, f * P:(f + 1) * P], xT[:, m, t * P:(t + 1) * P], ident[:])
                mm.then_inc(s_ft, 1)

            def first_results():
                for n in range(4):
                    result(n)

            down(1, U_DOWN2, 3, 4, first_results)
            for n in range(4, 8):
                result(n)


_INS = ["x", "norm1_g", "w_in", "q_norm_g", "k_norm_g", "conv_dw_w", "conv_dw_b", "conv_ln_g", "conv_ln_b", "w_out",
        "norm2_g", "w_up", "ffn_dw_w", "ffn_dw_b", "w_down", "norm_mix_w_2", "w_in_2", "b_attn_2", "lb_logits_2",
        "hg_norm_w_2", "sinks_2", "w_out_2", "norm_ffn_w_2", "w_gate_2", "w_up_2", "conv_w_2", "conv_b_2",
        "w_down_2", "final_norm_w_2"]


def kernel(**inputs):
    import numpy as np
    import concourse.bacc as bacc
    from concourse.bass_utils import run_bass_kernel_spmd

    nc = bacc.Bacc("TRN2", target_bir_lowering=False, num_devices=1)
    arrays, args = {}, []
    for name in _INS:
        a = np.ascontiguousarray(inputs[name])
        arrays[f"in_{name}"] = a
        args.append(nc.dram_tensor(f"in_{name}", a.shape, mybir.dt.from_np(a.dtype), kind="ExternalInput").ap())
    args.append(nc.dram_tensor("out_dram", (1, SEQ, DM), F32, kind="ExternalOutput").ap())
    hybrid_blocks_kernel(nc, *args)
    r = run_bass_kernel_spmd(nc, [arrays], core_ids=[0])
    return r.results[0]["out_dram"]
```
